# Optimizing a Trainium2 kernel written in Bass

```python
import math
import jax, jax.numpy as jnp
from jax import lax
import numpy as np

D_MODEL = 2048
BATCH = 1
SEQ = 256
DEPTH = 1

D_MIX = D_MODEL
SSM_WIDTH = D_MIX // 2
SSM_GROUP = 16
SSM_GROUPS = SSM_WIDTH // SSM_GROUP
SSM_STATE = 64
NSA_WIDTH = D_MIX - SSM_WIDTH
HEAD_DIM = 64
NSA_HEADS = NSA_WIDTH // HEAD_DIM
KV_HEADS = 4
Q_PER_KV = NSA_HEADS // KV_HEADS
KV_WIDTH = KV_HEADS * HEAD_DIM
CMP_BLOCK = 32
CMP_STRIDE = 16
CMP_HIDDEN = 256
SLC_BLOCK = 64
SLC_TOPK = 16
WINDOW = 512
Q_BLOCK = 128
SLC_Q_BLOCK = 64
REL_BUCKETS = 32
REL_MAX_DIST = 128
D_FF = 4 * D_MODEL
EPS = 1e-6
NEG = -1e30
FORCED_SCORE = 1e4
D_IN = SSM_WIDTH + NSA_WIDTH + 6 * KV_WIDTH + 3 * NSA_HEADS

kernel_name = "hymba_s5_nsa_hybrid_block"

def rmsnorm(x, w):
    xf = x.astype(jnp.float32)
    y = xf * lax.rsqrt(jnp.mean(xf * xf, axis=-1, keepdims=True) + EPS)
    return (y * w.astype(jnp.float32)).astype(x.dtype)

def masked_softmax(logits, mask):
    p = jax.nn.softmax(jnp.where(mask, logits, NEG), axis=-1)
    return p * jnp.any(mask, axis=-1, keepdims=True)

def rel_bucket(dist):
    dist = jnp.maximum(dist, 0)
    max_exact = REL_BUCKETS // 2
    large = max_exact + (jnp.log(jnp.maximum(dist, 1).astype(jnp.float32) / max_exact)
                         / math.log(REL_MAX_DIST / max_exact) * (REL_BUCKETS - max_exact)).astype(jnp.int32)
    large = jnp.minimum(large, REL_BUCKETS - 1)
    return jnp.where(dist < max_exact, dist, large)

def s5_mixer(u, a_re, a_im, log_dt, b_re, b_im, c_re, c_im, d, w_glu, b_glu):
    bsz, L, _ = u.shape
    ug = u.reshape(bsz, L, SSM_GROUPS, SSM_GROUP)
    dt = jnp.exp(log_dt)[:, None]
    mag = jnp.exp(dt * a_re)
    abar_re = mag * jnp.cos(dt * a_im)
    abar_im = mag * jnp.sin(dt * a_im)
    den = a_re * a_re + a_im * a_im
    zr, zi = abar_re - 1.0, abar_im
    coef_re = (zr * a_re + zi * a_im) / den
    coef_im = (zi * a_re - zr * a_im) / den
    bu_re = jnp.einsum('blgh,gph->blgp', ug, b_re)
    bu_im = jnp.einsum('blgh,gph->blgp', ug, b_im)
    xb_re = coef_re * bu_re - coef_im * bu_im
    xb_im = coef_re * bu_im + coef_im * bu_re
    ar = jnp.broadcast_to(abar_re, xb_re.shape)
    ai = jnp.broadcast_to(abar_im, xb_re.shape)

    def combine(e1, e2):
        a1r, a1i, b1r, b1i = e1
        a2r, a2i, b2r, b2i = e2
        return (a1r * a2r - a1i * a2i, a1r * a2i + a1i * a2r,
                a2r * b1r - a2i * b1i + b2r, a2r * b1i + a2i * b1r + b2i)

    _, _, s_re, s_im = lax.associative_scan(combine, (ar, ai, xb_re, xb_im), axis=1)
    y = (jnp.einsum('blgp,ghp->blgh', s_re, c_re) - jnp.einsum('blgp,ghp->blgh', s_im, c_im)
         + d * ug).reshape(bsz, L, SSM_WIDTH)
    z = jax.nn.gelu(y)
    return z * jax.nn.sigmoid(z @ w_glu + b_glu)

def compress(k, idx, pe, w1, w2):
    bsz = k.shape[0]
    n_cmp = idx.shape[0]
    blocks = k[:, idx] + pe[None, None, :, None, :]
    flat = blocks.transpose(0, 1, 3, 2, 4).reshape(bsz, n_cmp, KV_HEADS, CMP_BLOCK * HEAD_DIM)
    return jax.nn.gelu(flat @ w1) @ w2

def nsa_mixer(q, kc, vc, ks, vs, kw, vw, gate_logits, pe_ck, w_ck1, w_ck2, pe_cv, w_cv1, w_cv2, rel_table):
    bsz, L, _ = q.shape
    q = q.reshape(bsz, L, KV_HEADS, Q_PER_KV, HEAD_DIM) * (HEAD_DIM ** -0.5)
    kc, vc, ks, vs, kw, vw = [t.reshape(bsz, L, KV_HEADS, HEAD_DIM) for t in (kc, vc, ks, vs, kw, vw)]
    pos = jnp.arange(L)
    table_g = rel_table.reshape(REL_BUCKETS, KV_HEADS, Q_PER_KV).transpose(1, 0, 2)
    g_ix = jnp.arange(KV_HEADS)[None, :, None, None]
    b_ix = jnp.arange(bsz)[:, None, None, None]

    n_cmp = (L - CMP_BLOCK) // CMP_STRIDE + 1
    cmp_idx = np.arange(n_cmp)[:, None] * CMP_STRIDE + np.arange(CMP_BLOCK)[None, :]
    k_cmp = compress(kc, cmp_idx, pe_ck, w_ck1, w_ck2)
    v_cmp = compress(vc, cmp_idx, pe_cv, w_cv1, w_cv2)
    dist_c = pos[:, None] - jnp.asarray(cmp_idx[:, -1])[None, :]
    bias_c = table_g[:, rel_bucket(dist_c)].transpose(0, 3, 1, 2)
    logits_c = jnp.einsum('blgrd,bngd->bgrln', q, k_cmp).astype(jnp.float32) + bias_c
    p_c = masked_softmax(logits_c, dist_c >= 0)
    o_cmp = jnp.einsum('bgrln,bngd->blgrd', p_c.astype(v_cmp.dtype), v_cmp)

    n_slc = L // SLC_BLOCK
    overlap = ((cmp_idx[:, :, None] // SLC_BLOCK) == np.arange(n_slc)[None, None, :]).sum(1) / CMP_BLOCK
    imp = jnp.einsum('bgrln,ns->bgls', p_c, jnp.asarray(overlap, dtype=jnp.float32))
    cur = pos // SLC_BLOCK
    blk = jnp.arange(n_slc)
    forced = (blk[None, :] == 0) | (blk[None, :] == cur[:, None]) | (blk[None, :] == cur[:, None] - 1)
    valid = blk[None, :] <= cur[:, None]
    score = jnp.where(forced, FORCED_SCORE, jnp.where(valid, imp, -1.0))
    n_top = min(SLC_TOPK, n_slc)
    _, sel = lax.top_k(score, n_top)

    ks_g = ks.reshape(bsz, n_slc, SLC_BLOCK, KV_HEADS, HEAD_DIM).transpose(0, 3, 1, 2, 4)
    vs_g = vs.reshape(bsz, n_slc, SLC_BLOCK, KV_HEADS, HEAD_DIM).transpose(0, 3, 1, 2, 4)
    n_qb = L // SLC_Q_BLOCK
    q_blocks = q.reshape(bsz, n_qb, SLC_Q_BLOCK, KV_HEADS, Q_PER_KV, HEAD_DIM).transpose(1, 0, 2, 3, 4, 5)
    sel_blocks = sel.reshape(bsz, KV_HEADS, n_qb, SLC_Q_BLOCK, n_top).transpose(2, 0, 1, 3, 4)
    pos_blocks = pos.reshape(n_qb, SLC_Q_BLOCK)
    n_tok = n_top * SLC_BLOCK

    def slc_block(args):
        qb_, selb, posb = args
        kg = ks_g[b_ix, g_ix, selb].reshape(bsz, KV_HEADS, SLC_Q_BLOCK, n_tok, HEAD_DIM)
        vg = vs_g[b_ix, g_ix, selb].reshape(bsz, KV_HEADS, SLC_Q_BLOCK, n_tok, HEAD_DIM)
        tok = (selb[..., None] * SLC_BLOCK + jnp.arange(SLC_BLOCK)).reshape(bsz, KV_HEADS, SLC_Q_BLOCK, n_tok)
        dist = posb[None, None, :, None] - tok
        bias = table_g[g_ix, rel_bucket(dist)].transpose(0, 1, 4, 2, 3)
        logits = jnp.einsum('bqgrd,bgqtd->bgrqt', qb_, kg).astype(jnp.float32) + bias
        p = masked_softmax(logits, (dist >= 0)[:, :, None])
        return jnp.einsum('bgrqt,bgqtd->bqgrd', p.astype(vg.dtype), vg)

    o_slc = lax.map(slc_block, (q_blocks, sel_blocks, pos_blocks))
    o_slc = o_slc.transpose(1, 0, 2, 3, 4, 5).reshape(bsz, L, KV_HEADS, Q_PER_KV, HEAD_DIM)

    n_wb = L // Q_BLOCK
    span = WINDOW + Q_BLOCK
    key_idx = np.arange(n_wb)[:, None] * Q_BLOCK + np.arange(span)[None, :]
    kw_pad = jnp.pad(kw, ((0, 0), (WINDOW, 0), (0, 0), (0, 0)))
    vw_pad = jnp.pad(vw, ((0, 0), (WINDOW, 0), (0, 0), (0, 0)))
    kwin = kw_pad[:, key_idx]
    vwin = vw_pad[:, key_idx]
    qw = q.reshape(bsz, n_wb, Q_BLOCK, KV_HEADS, Q_PER_KV, HEAD_DIM)
    kpos = jnp.asarray(key_idx - WINDOW)
    qpos = pos.reshape(n_wb, Q_BLOCK)
    dist_w = qpos[:, :, None] - kpos[:, None, :]
    mask_w = (dist_w >= 0) & (dist_w < WINDOW) & (kpos[:, None, :] >= 0)
    bias_w = table_g[:, rel_bucket(dist_w)].transpose(1, 0, 4, 2, 3)
    logits_w = jnp.einsum('bnqgrd,bnkgd->bngrqk', qw, kwin).astype(jnp.float32) + bias_w
    p_w = masked_softmax(logits_w, mask_w[:, None, None])
    o_win = jnp.einsum('bngrqk,bnkgd->bnqgrd', p_w.astype(vwin.dtype), vwin)
    o_win = o_win.reshape(bsz, L, KV_HEADS, Q_PER_KV, HEAD_DIM)

    g = jax.nn.sigmoid(gate_logits.reshape(bsz, L, KV_HEADS, Q_PER_KV, 3))
    o = g[..., 0:1] * o_cmp + g[..., 1:2] * o_slc + g[..., 2:3] * o_win
    return o.reshape(bsz, L, NSA_WIDTH)

def setup_inputs(seed: int = 0) -> dict:
    key = jax.random.key(seed)
    ks = jax.random.split(key, 26)
    nrm = jax.random.normal
    f32 = jnp.float32
    x = nrm(ks[0], (BATCH, SEQ, D_MODEL), f32)
    norm1_w = 1.0 + 0.01 * nrm(ks[1], (DEPTH, D_MODEL), f32)
    w_in = nrm(ks[2], (DEPTH, D_MODEL, D_IN), f32) * D_MODEL ** -0.5
    ssm_a_re = -0.5 * jnp.exp(0.02 * nrm(ks[3], (DEPTH, SSM_GROUPS, SSM_STATE), f32))
    ssm_a_im = (math.pi * jnp.arange(SSM_STATE, dtype=f32))[None, None, :] + 0.01 * nrm(ks[4], (DEPTH, SSM_GROUPS, SSM_STATE), f32)
    ssm_log_dt = jax.random.uniform(ks[5], (DEPTH, SSM_GROUPS), f32, math.log(1e-3), math.log(1e-1))
    ssm_b_re = nrm(ks[6], (DEPTH, SSM_GROUPS, SSM_STATE, SSM_GROUP), f32) * (2 * SSM_GROUP) ** -0.5
    ssm_b_im = nrm(ks[7], (DEPTH, SSM_GROUPS, SSM_STATE, SSM_GROUP), f32) * (2 * SSM_GROUP) ** -0.5
    ssm_c_re = nrm(ks[8], (DEPTH, SSM_GROUPS, SSM_GROUP, SSM_STATE), f32) * (2 * SSM_STATE) ** -0.5
    ssm_c_im = nrm(ks[9], (DEPTH, SSM_GROUPS, SSM_GROUP, SSM_STATE), f32) * (2 * SSM_STATE) ** -0.5
    ssm_d = nrm(ks[10], (DEPTH, SSM_GROUPS, SSM_GROUP), f32)
    w_glu = nrm(ks[11], (DEPTH, SSM_WIDTH, SSM_WIDTH), f32) * SSM_WIDTH ** -0.5
    b_glu = 0.01 * nrm(ks[12], (DEPTH, SSM_WIDTH), f32)
    pe_ck = 0.1 * nrm(ks[13], (DEPTH, CMP_BLOCK, HEAD_DIM), f32)
    w_ck1 = nrm(ks[14], (DEPTH, CMP_BLOCK * HEAD_DIM, CMP_HIDDEN), f32) * (CMP_BLOCK * HEAD_DIM) ** -0.5
    w_ck2 = nrm(ks[15], (DEPTH, CMP_HIDDEN, HEAD_DIM), f32) * CMP_HIDDEN ** -0.5
    pe_cv = 0.1 * nrm(ks[16], (DEPTH, CMP_BLOCK, HEAD_DIM), f32)
    w_cv1 = nrm(ks[17], (DEPTH, CMP_BLOCK * HEAD_DIM, CMP_HIDDEN), f32) * (CMP_BLOCK * HEAD_DIM) ** -0.5
    w_cv2 = nrm(ks[18], (DEPTH, CMP_HIDDEN, HEAD_DIM), f32) * CMP_HIDDEN ** -0.5
    w_out = nrm(ks[19], (DEPTH, D_MIX, D_MODEL), f32) * D_MIX ** -0.5
    norm2_w = 1.0 + 0.01 * nrm(ks[20], (DEPTH, D_MODEL), f32)
    w_up = nrm(ks[21], (DEPTH, D_MODEL, D_FF), f32) * D_MODEL ** -0.5
    w_down = nrm(ks[22], (DEPTH, D_FF, D_MODEL), f32) * D_FF ** -0.5
    rel_table = 0.5 * nrm(ks[23], (REL_BUCKETS, NSA_HEADS), f32)
    norm_f_w = 1.0 + 0.01 * nrm(ks[24], (D_MODEL,), f32)
    return {"x": x, "norm1_w": norm1_w, "w_in": w_in, "ssm_a_re": ssm_a_re, "ssm_a_im": ssm_a_im,
            "ssm_log_dt": ssm_log_dt, "ssm_b_re": ssm_b_re, "ssm_b_im": ssm_b_im, "ssm_c_re": ssm_c_re,
            "ssm_c_im": ssm_c_im, "ssm_d": ssm_d, "w_glu": w_glu, "b_glu": b_glu, "pe_ck": pe_ck,
            "w_ck1": w_ck1, "w_ck2": w_ck2, "pe_cv": pe_cv, "w_cv1": w_cv1, "w_cv2": w_cv2,
            "w_out": w_out, "norm2_w": norm2_w, "w_up": w_up, "w_down": w_down,
            "rel_table": rel_table, "norm_f_w": norm_f_w}

def reference(x, norm1_w, w_in, ssm_a_re, ssm_a_im, ssm_log_dt, ssm_b_re, ssm_b_im, ssm_c_re, ssm_c_im,
              ssm_d, w_glu, b_glu, pe_ck, w_ck1, w_ck2, pe_cv, w_cv1, w_cv2, w_out, norm2_w, w_up, w_down,
              rel_table, norm_f_w):
    sizes = [SSM_WIDTH, NSA_WIDTH] + [KV_WIDTH] * 6
    offsets = np.cumsum(sizes).tolist()
    for l in range(DEPTH):
        h = rmsnorm(x, norm1_w[l])
        proj = h @ w_in[l]
        u, q, kc, vc, ks_, vs_, kw, vw, gl = jnp.split(proj, offsets, axis=-1)
        y_ssm = s5_mixer(u, ssm_a_re[l], ssm_a_im[l], ssm_log_dt[l], ssm_b_re[l], ssm_b_im[l],
                         ssm_c_re[l], ssm_c_im[l], ssm_d[l], w_glu[l], b_glu[l])
        y_nsa = nsa_mixer(q, kc, vc, ks_, vs_, kw, vw, gl, pe_ck[l], w_ck1[l], w_ck2[l],
                          pe_cv[l], w_cv1[l], w_cv2[l], rel_table)
        x = x + jnp.concatenate([y_ssm, y_nsa], axis=-1) @ w_out[l]
        h = rmsnorm(x, norm2_w[l])
        x = x + jnp.square(jax.nn.relu(h @ w_up[l])) @ w_down[l]
    return rmsnorm(x, norm_f_w)


_drawn_inputs = setup_inputs


def setup_inputs(seed=0):
    import zlib

    import numpy as np

    out = dict(_drawn_inputs(seed))
    spreads = {}
    factors = {'norm1_w': 8.0,
     'ssm_a_re': 64.0,
     'ssm_a_im': 28.304,
     'ssm_log_dt': 29.2,
     'ssm_b_re': 39.432,
     'ssm_b_im': 39.808,
     'ssm_c_re': 39.456,
     'ssm_c_im': 39.616,
     'b_glu': 64.0,
     'pe_ck': 8.0,
     'norm2_w': 32.598,
     'norm_f_w': 31.781,
     'pe_cv': 8.0}
    for name, (base, spread) in spreads.items():
        noise = np.random.default_rng([zlib.crc32(name.encode()), seed]).standard_normal(out[name].shape)
        drawn = base * np.exp(spread * noise) if base else spread * noise
        out[name] = __import__('jax').numpy.asarray(drawn.astype(out[name].dtype))
    for name, factor in factors.items():
        out[name] = (out[name] * factor).astype(out[name].dtype)
    return out
```

```python
import math
from contextlib import ExitStack

import numpy as np

import concourse.bass as bass
from concourse import mybir

SEQ, D = 256, 2048
TILES = SEQ // 128
KT = D // 128
HEADS, HD, KV = 16, 64, 4
D_IN = 3632
N_CMP, CMP_PAD = 15, 16
D_FF = 4 * D
FF_HALF = D_FF // 2
PAIRS, OCTETS = 32, 8
BUCKETS, MAX_DIST = 32, 128
EPS = 1e-6
NEG = -1e30
MAGIC = 12582912.0
TWO_PI_DOWN = 6.283185
INV_2PI = 1.0 / (2.0 * math.pi)
C1, C2 = 6.28125, 0.001934051513671875
C3 = 2.0 * math.pi - C1 - C2

PACK = {}
_at = 0
for _n, _w in (("n1", 16), ("n2", 16), ("are", 32), ("aim", 32), ("ldt", 32), ("d", 8), ("bglu", 8),
               ("pek", 16), ("pev", 16), ("w2k", 256), ("w2v", 128), ("tv", 256), ("ident", 128),
               ("valid", 2)):
    PACK[_n] = (_at, _at + _w)
    _at += _w
PACK_W = _at
BIAS_W = 384
DIST_W = 768


def hybrid_layer(nc, x, w_in, w_glu, w_out, w_up, w_down, w_ck1, w_cv1, nf, params, bc, buckets, out):
    fp32, f32r = mybir.dt.float32, mybir.dt.float32r
    ACT, ALU, AX = mybir.ActivationFunctionType, mybir.AluOpType, mybir.AxisListType

    x_v = x.rearrange("(t p) n -> p t n", p=128)
    out_v = out.rearrange("(t p) n -> p t n", p=128)
    BIAS_PITCH = 128 * (BIAS_W + 1)
    bias_dram = nc.dram_tensor("bias_rows", [HEADS, BIAS_PITCH], fp32, kind="Internal").ap()

    IN_CHUNKS = [0, 1, 4, 2, 3, 5, 6]
    STREAM = []

    def four(kind, c):
        STREAM.extend((kind, c, g) for g in range(4))

    for c in range(4):
        four("in", c)
    STREAM.extend(("cmp", c // 2, c % 2) for c in range(4))
    four("in", 4)
    STREAM.append(("gate", 0, 0))
    four("in", 5)
    four("in", 6)
    for c in range(2):
        STREAM.extend(("glu", c, g) for g in range(2))
    for c in range(4):
        four("out", c)
    N0 = len(STREAM)
    is_split = [k != "cmp" for k, _, _ in STREAM]
    split_no = [sum(is_split[:s]) for s in range(N0)]
    SP0 = sum(is_split)
    first_piece = {}
    for _s, (_k, _c, _g) in enumerate(STREAM):
        first_piece.setdefault((_k, _c), _s)
    SLOTS = 4

    def width(s):
        return KT * 48 if STREAM[s][0] == "gate" else 2048


    ctx = ExitStack()
    with ctx:
        BASE = 16512
        K = 1024

        def at(name, shape, dt, off):
            return nc.alloc_sbuf_tensor_at(name, shape, dt, offset=BASE + int(off * K))

        def sem(name):
            return ctx.enter_context(nc.semaphore(name))

        raw = [at(f"raw{i}", [128, 2048], fp32, 8 * i) for i in range(SLOTS)]
        wlo = [at(f"wlo{i}", [128, 2048], f32r, 8 * i) for i in range(SLOTS)]
        whi = [at(f"whi{i}", [128, 2048], f32r, 32 + 8 * i) for i in range(2)]
        AH = at("act_hi", [128, KT, 256], f32r, 48)
        AL = at("act_lo", [128, KT, 256], f32r, 64)
        X = at("x_rows", [128, TILES, D], fp32, 80)
        ynsa = at("y_nsa", [128, TILES, 1024], fp32, 80)
        vblk = at("v_cmp_blocks", [128, KV, 256], fp32, 88)
        pcT = at("p_cmp_T", [128, TILES * KV, 128], fp32, 92)
        pcmp = at("p_cmp", [128, TILES * HEADS, 32], fp32, 92)
        prob = [at(f"prob{i}", [128, 2, 384], fp32, 96 + 3 * i) for i in range(2)]
        pT = [at(f"prob_T{i}", [128, 2, 384], fp32, 102 + 3 * i) for i in range(2)]
        lg = [at("logits0", [128, 2, 384], fp32, 108), at("logits1", [128, 2, 384], fp32, 152)]
        BL = at("b_T", [128, OCTETS, 2, 128], fp32, 96)
        CL = at("c_blocks", [128, 2, PAIRS, 32], fp32, 104)
        CS = [at(f"cos_sin{i}", [128, 2, 2, 256], fp32, 112 + 4 * i) for i in range(2)]
        turn = at("turns", [128, 2, 256], fp32, 120)
        whole = at("whole_turns", [128, 2, 256], fp32, 122)
        mixv = [at("mix0", [128, 4, 256], fp32, 120), at("mix1", [128, 4, 256], fp32, 112)]
        uT = at("u_T", [128, OCTETS, 256], fp32, 124)
        qT = at("q_T", [128, 8, 256], fp32, 132)
        junk = [at(f"junk{i}", [128, 1024], fp32, 124 + 4 * i) for i in range(2)]
        kdup = [at(f"k_dup{a}", [128, KV, 256], fp32, 140 + 4 * a) for a in range(2)]
        vrow = [at(f"v_rows{a}", [128, TILES, 256], fp32, 148 + 2 * a) for a in range(2)]
        kcat = at("k_cat", [128, 2 * KV * 128 + 8], fp32, 152)
        hrow = at("hidden_rows", [64, 512], fp32, 152)
        diag = at("row_scales", [128, TILES, 128], fp32, 140)
        flat = at("blocks_flat", [128, 2, KT, 64], fp32, 140)
        hidk = at("hidden_k", [128, 2, KV, 32], fp32, 156.25)
        hidv = at("hidden_v", [128, 2, KV, 4, 32], fp32, 148)
        o = 157.25

        def small(name, shape):
            nonlocal o
            n = 4 * int(np.prod(shape[1:]))
            n = (n + 31) // 32 * 32
            t = at(name, shape, fp32, o)
            o += n / K
            return t

        gates = small("gates", [128, TILES, 48])
        kcmp = small("k_cmp_T", [128, KV, 32])
        nmax = [small(f"neg_max{i}", [128, 4]) for i in range(2)]
        esum = [small(f"exp_sum{i}", [128, 4]) for i in range(2)]
        alpha = [small(f"alpha{i}", [128, 2, 4]) for i in range(2)]
        cst = small("cmp_stats", [128, 4, TILES * HEADS])
        assert o <= 160
        par = at("params", [128, PACK_W], fp32, 160)
        assert PACK_W * 4 <= 4 * K
        bcr = at("b_c_raw", [128, 4, PAIRS, 16], fp32, 164)
        BD = at("b_blocks", [128, 2, PAIRS, 32], fp32, 172)
        bias = at("bias_neg", [128, HEADS, 256], fp32, 164)
        biasc = at("bias_cmp_neg", [128, TILES, HEADS, CMP_PAD], fp32, 180)
        M = at("rot_prod", [128, 2, 2, 256], fp32, 182)
        W = at("rot_in", [128, 2, 256], fp32, 186)
        Z = [at(f"scan{i}", [128, 2, 256], fp32, 188 + 2 * i) for i in range(2)]
        N = [at(f"back_prod{i}", [128, 2, 2, 256], fp32, 192 + 4 * i) for i in range(2)]
        S = [at(f"state{i}", [128, 2, 256], fp32, 200 + 2 * i) for i in range(2)]
        T = [at(f"o_scaled{i}", [128, 2, TILES, HD], fp32, 204 + i) for i in range(2)]
        ZH = at("z_hi", [128, OCTETS, 256], f32r, 182)
        ZL = at("z_lo", [128, OCTETS, 256], f32r, 190)
        oh = at("buckets", [BUCKETS + 1, DIST_W + BIAS_W + HEADS], fp32, 192)
        brow = at("bias_row", [HEADS, BIAS_W], fp32, 198)
        lcmp = biasc[:, :, :, :].rearrange("p t h n -> p (t h) n")
        coef = at("coefs", [128, 12, PAIRS], fp32, 182)
        bprod = at("b_prod", [128, 4, PAIRS, 16], fp32, 184)
        st = at("ssm_stay", [128, 2, PAIRS], fp32, 206)
        spare = at("spare", [128, 3], fp32, 206.375)
        rs = at("row_stats", [128, 3, 2], fp32, 206.5)
        parts = at("row_parts", [128, TILES, 4], fp32, 206.625)
        MH = at("mlp_hi", [128, 32, 256], f32r, 96)
        ML = at("mlp_lo", [128, 32, 256], f32r, 128)
        RT = [at(f"relu{i}", [128, 4, 256], fp32, 164 + 4 * i) for i in range(2)]
        SQ = [at(f"squared{i}", [128, 4, 256], fp32, 172 + 4 * i) for i in range(2)]
        NF = at("norm_f", [128, D], fp32, 182)
        junk_mlp = at("junk_mlp", [128, 512], fp32, 164)

        def P(name):
            return par[:, PACK[name][0]:PACK[name][1]]

        ident = P("ident")
        tv = P("tv")

        G = [ctx.enter_context(nc.psum_tensor(f"gemm{i}", [128, 2, 512], fp32)) for i in range(2)]
        BU = [ctx.enter_context(nc.psum_tensor(f"bu{i}", [128, 2, 256], fp32)) for i in range(2)]
        OB = ctx.enter_context(nc.psum_tensor("o_bank", [128, 512], fp32))
        YB = ctx.enter_context(nc.psum_tensor("y_bank", [128, 512], fp32))
        hid_ps = OB[0:64, :]
        TB = [BU[0][:, :, :].rearrange("p a b -> p (a b)"), BU[1][:, :, :].rearrange("p a b -> p (a b)"),
              OB[:, :], YB[:, :]]
        kc_ps = OB[:, 0:128]
        vc_ps = OB[:, 128:384].rearrange("p (v d) -> p v d", v=KV)
        CMP_O = [G[0][:, 0, :], G[0][:, 1, :], OB[:, :], G[0][:, 0, :]]
        o_ps = OB[:, 0:256].rearrange("p (a t d) -> p a t d", a=2, t=2)

        piece_in = [sem(f"piece_in{i}") for i in range(SLOTS)]
        x_in = [sem(f"x_in{i}") for i in range(4)]
        par_in, bc_in, oh_in, nf_in = (sem(n) for n in ("par_in", "bc_in", "oh_in", "nf_in"))
        hi_ready, lo_ready, piece_used = sem("hi_ready"), sem("lo_ready"), sem("piece_used")
        bias_row_ready, bias_out, bias_in, biasc_ready = (sem(n) for n in (
            "bias_row_ready", "bias_out", "bias_in", "biasc_ready"))
        bias_mm, zeroed, coef_step, coef_act = (sem(n) for n in ("bias_mm", "zeroed", "coef_step", "coef_act"))
        b_prod, b_blocks, b_T, b_T_out, c_blocks = (sem(n) for n in (
            "b_prod_done", "b_blocks_done", "b_T_done", "b_T_out", "c_blocks_done"))
        ss_ready, std_ready, rinv_ready, diag_ready = (sem(n) for n in (
            "ss_ready", "std_ready", "rinv_ready", "diag_ready"))
        own_sums = sem("own_sums")
        sum_ready, root_loaded = sem("sum_ready"), sem("root_loaded")
        h_tr, h_hi, h_lo = sem("h_tr"), sem("h_hi"), sem("h_lo")
        u_ready, kc_ready, q_ready, gate_ready, kv_ready = (sem(n) for n in (
            "u_ready", "kc_ready", "q_ready", "gate_ready", "kv_ready"))
        tab_work, tab_frac, tab_trig = sem("tab_work"), sem("tab_frac"), sem("tab_trig")
        bu_done, ssm_prod, ssm_rot, ssm_scan, ssm_back, ssm_state, y_done, y_out = (sem(n) for n in (
            "bu_done", "ssm_prod", "ssm_rot", "ssm_scan", "ssm_back", "ssm_state", "y_done", "y_out"))
        hidv_zero, cmp_zeroed = sem("hidv_zero"), sem("cmp_zeroed")
        flat_ready, hrow_ready, hid_T, pads = (sem(n) for n in ("flat_ready", "hrow_ready", "hid_T", "pads_zeroed"))
        hid_ready, cmp_kv, cmp_kv_out = (sem(n) for n in ("hid_ready", "cmp_kv", "cmp_kv_out"))
        cmp_logits, cmp_step, cmp_exp, cmp_T, cmp_T_out, cmp_o, cmp_o_out = (sem(n) for n in (
            "cmp_logits", "cmp_step", "cmp_exp", "cmp_T", "cmp_T_out", "cmp_o", "cmp_o_out"))
        qk_done, lg_ready, exp_ready, pT_done, pT_out, pv_done = (sem(n) for n in (
            "qk_done", "lg_ready", "exp_ready", "pT_done", "pT_out", "pv_done"))
        al_step, o_scaled, y_added = sem("al_step"), sem("o_scaled_done"), sem("y_added")
        yt_done, yt_hi, yt_lo = sem("yt_done"), sem("yt_hi"), sem("yt_lo")
        z_ready, z_hi, z_lo = sem("z_ready"), sem("z_hi_done"), sem("z_lo_done")
        sg_ready, mix_ready, mix_hi, mix_lo = (sem(n) for n in ("sg_ready", "mix_ready", "mix_hi", "mix_lo"))
        x_added = sem("x_added")
        relu_ready, sq_ready, mlp_hi, mlp_lo = (sem(n) for n in ("relu_ready", "sq_ready", "mlp_hi_done", "mlp_lo_done"))
        gained = sem("gained")
        fin_step, stored = sem("fin_step"), sem("stored")

        STEPS = []

        def pair_slot(k):
            if k % 2 == 0 and k // 2 + 1 < PAIRS // 2:
                STEPS.append(("tab", k // 2 + 1))
            if k % 2 == 1 and k // 2 + 1 < PAIRS // 2:
                STEPS.append(("trig", k // 2 + 1))
            if k + 1 < PAIRS:
                STEPS.append(("bu", k + 1))
            if k < PAIRS:
                STEPS.append(("rot", k))
                STEPS.append(("back", k))
            if 1 <= k <= PAIRS:
                STEPS.append(("state", k - 1))
            if k >= 2 and k - 2 < PAIRS:
                STEPS.append(("y", k - 2))

        slots = iter(range(PAIRS + 2))
        PROD = [("in", c) for c in range(5)] + [("gate", 0), ("in", 5), ("in", 6)]
        prod_no = {p: i for i, p in enumerate(PROD)}
        AFTER = {("in", 0, 0): [("coef_trig", 0)], ("in", 0, 1): [("coef", 0)], ("in", 0, 2): [("c_blocks", 0)],
                 ("in", 0, 3): [("b_blocks", 0), ("tab", 0), ("b_T", 0)],
                 }
        SLOT_END = {("in", 4, 0): [("hidden", 0), ("hid_T", 0)],
                    ("in", 4, 1): [("hid_T_out", 0), ("cmp_kv", 0)], ("in", 4, 2): [("cmp_kv_out", 0)],
                    ("gate", 0, 0): [("cmp_l", 0)], ("in", 5, 0): [("cmp_l_out", 0), ("cmp_l", 1)],
                    ("in", 5, 1): [("cmp_l_out", 1), ("cmp_min", 0)],
                    ("in", 5, 2): [("cmp_exp", 0), ("cmp_p", 0)],
                    ("in", 6, 0): [("cmp_T", 0)],
                    ("in", 6, 1): [("cmp_T_out", 0), ("cmp_o", 0), ("cmp_o", 1), ("cmp_o", 2)],
                    ("in", 6, 2): [("cmp_o_out", 0), ("cmp_o_out", 1), ("cmp_o_out", 2), ("cmp_o", 3)],
                    ("in", 6, 3): [("cmp_o_out", 3), ("gelu", 0), ("gelu", 1), ("gelu", 2)]}
        pending = None
        for s, (kind, c, g) in enumerate(STREAM):
            if kind == "glu":
                break
            STEPS.extend([("split", s), ("product", s)])
            if kind != "cmp" and pending is not None:
                STEPS.append(("evac", pending))
                if pending == 0:
                    STEPS.append(("trig", 0))
                    STEPS.append(("bu", 0))
                if pending == 2:
                    STEPS.append(("flat", 0))
                pending = None
            STEPS.extend(AFTER.get((kind, c, g), []))
            if kind == "gate" or (kind == "in" and g == 3):
                pending = prod_no[(kind, c)]
            for _ in range(0 if s < 5 else 2 if kind == "cmp" else 1):
                k = next(slots, None)
                if k is not None:
                    pair_slot(k)
            STEPS.extend(SLOT_END.get((kind, c, g), []))
        STEPS.append(("evac", pending))
        for k in slots:
            pair_slot(k)
        G0, O0 = first_piece[("glu", 0)], first_piece[("out", 0)]
        def split(s):
            STEPS.append(("split", s))

        AT_HEAD = {h: G0 + h - 2 for h in range(2, 6)}
        AT_HEAD.update({12: O0, 14: O0 + 1})
        STEPS.append(("gelu", 3))
        STEPS.append(("qk", 0))
        STEPS.append(("z", 0))
        for h in range(1, HEADS + 2):
            if h + 1 in AT_HEAD:
                split(AT_HEAD[h + 1])
            if h < HEADS:
                STEPS.append(("qk", h))
            if h <= HEADS:
                STEPS.append(("pT", h - 1))
            if h >= 2:
                STEPS.append(("pv", h - 2))
            if h >= 5 and h % 2 == 1:
                STEPS.append(("yT", (h - 5) // 2))
            if h in AT_HEAD:
                STEPS.append(("product", AT_HEAD[h]))
            if h in (4, 6):
                STEPS.append(("glu_gate", (h - 4) // 2))
            if h in (5, 7):
                STEPS.append(("glu_mix", (h - 5) // 2))
            if h == HEADS:
                split(O0 + 2)
        STEPS.append(("product", O0 + 2))
        split(O0 + 3)
        STEPS.append(("yT", 7))
        STEPS.append(("product", O0 + 3))
        for s in range(O0 + 4, O0 + 16):
            split(s)
            STEPS.append(("product", s))
            if (s - O0) % 4 == 0:
                STEPS.append(("add", (s - O0) // 4 - 1))
        STEPS.append(("add", 3))

        EVAC = {0: (u_ready, 2), 1: (u_ready, 4), 2: (kc_ready, 4), 3: (q_ready, 2), 4: (q_ready, 4),
                5: (gate_ready, 1), 6: (kv_ready, 5), 7: (kv_ready, 10)}

        block = ctx.enter_context(nc.Block())

        def compress_layout(copy, b, half):
            v = b[64 * half:64 * half + 64, :, :].rearrange("p a (m t q) -> p (a m) t q", m=2, q=2)
            for par_ in range(2):
                copy(kcat[64 * par_:64 * par_ + 64, 0:1024].rearrange("p (k h t) -> p k h t", h=2, t=128)[:, :, half, :],
                     v[:, :, :, par_], kc_ready)

        def key_layout(copy, b, a, half):
            for to in range(2):
                copy(kdup[a][64 * to:64 * to + 64, half::2, :],
                     b[64 * half:64 * half + 64, 0, :].rearrange("p (m t) -> p m t", m=2), kv_ready)

        @block.sync
        def _(sp):
            for j in range(2):
                for t in range(TILES):
                    sp.dma_start(X[:, t, j * 1024:(j + 1) * 1024],
                                 x_v[:, t, j * 1024:(j + 1) * 1024]).then_inc(x_in[2 * j + t], 16)

            def source(kind, c, g):
                if kind == "in":
                    n = IN_CHUNKS[c]
                    return w_in[g * 512:(g + 1) * 512, n * 512:(n + 1) * 512].rearrange("(k p) n -> p k n", p=128)
                if kind == "gate":
                    return w_in[:, 3584:D_IN].rearrange("(k p) n -> p k n", p=128)
                if kind == "cmp":
                    w = (w_ck1, w_cv1)[c]
                    return w[g * 1024:(g + 1) * 1024, :].rearrange("(k p) n -> p k n", p=128)
                w = w_glu if kind == "glu" else w_out
                return w[g * 512:(g + 1) * 512, c * 512:(c + 1) * 512].rearrange("(k p) n -> p k n", p=128)

            def load_piece(s):
                kind, c, g = STREAM[s]
                src = source(kind, c, g)
                if s >= SLOTS:
                    sp.wait_ge(piece_used, s - SLOTS + 1)
                n = src.shape[1] * src.shape[2]
                dst = raw[s % SLOTS][:, 0:n].rearrange("p (k n) -> p k n", n=src.shape[2])
                sp.dma_start(dst, src).then_inc(piece_in[s % SLOTS], 16)

            for s in range(N0):
                if s == O0 + 4:
                    sp.wait_ge(yt_done, 8)
                    for j in range(2):
                        for t in range(TILES):
                            sp.dma_start(X[:, t, j * 1024:(j + 1) * 1024],
                                         x_v[:, t, j * 1024:(j + 1) * 1024]).then_inc(x_in[2 * j + t], 16)
                load_piece(s)
                if s == 7:
                    sp.wait_ge(bias_out, 16)
                    sp.wait_ge(b_T_out, 4)
                    sp.wait_ge(c_blocks, 4)
                    sp.dma_start(bias[:, :, :], bass.AP(bias_dram.tensor, 127, [[BIAS_W, 128], [BIAS_PITCH, HEADS], [1, 256]])
                                 ).then_inc(bias_in, 16)
            sp.wait_ge(piece_used, first_piece[("glu", 1)] + 2)
            sp.dma_start(NF[:, :], nf.partition_broadcast(128)).then_inc(nf_in, 16)
            for f in range(2):
                up0 = N0 + 64 * f
                with sp.Fori(0, 8) as c:
                    for g in range(4):
                        slot = (up0 + g) % SLOTS
                        sp.wait_ge(piece_used, c * 4 + (up0 + g - SLOTS + 1))
                        sp.dma_start(raw[slot][:, :].rearrange("p (k n) -> p k n", n=512),
                                     w_up[g * 512:(g + 1) * 512, bass.ds(c * 512 + f * FF_HALF, 512)]
                                     .rearrange("(k p) n -> p k n", p=128)).then_inc(piece_in[slot], 16)
                dn0 = up0 + 32
                with sp.Fori(0, 4) as c:
                    for g in range(8):
                        slot = (dn0 + g) % SLOTS
                        sp.wait_ge(piece_used, c * 8 + (dn0 + g - SLOTS + 1))
                        sp.dma_start(raw[slot][:, :].rearrange("p (k n) -> p k n", n=512),
                                     w_down[f * FF_HALF + g * 512:f * FF_HALF + (g + 1) * 512, bass.ds(c * 512, 512)]
                                     .rearrange("(k p) n -> p k n", p=128)).then_inc(piece_in[slot], 16)
            for t in range(TILES):
                for j in range(2):
                    sp.wait_ge(fin_step, 2 * t + j + 1)
                    cols = slice(1024 * j, 1024 * j + 1024)
                    sp.dma_start(out_v[:, t, cols], X[:, t, cols]).then_inc(stored, 16)
            sp.wait_ge(stored, 16 * 2 * TILES)

        @block.gpsimd
        def _(pool):
            pool.memset(CL[:, :, :, :], 0.0).then_inc(zeroed, 1)
            pool.memset(BD[:, :, :, :], 0.0).then_inc(zeroed, 1)
            pool.memset(hidk[:, :, :, :], 0.0).then_inc(zeroed, 1)
            pool.memset(kcat[:, 1024:1032], 0.0).then_inc(pads, 1)
            pool.memset(hidv[:, :, :, :, :], 0.0).then_inc(hidv_zero, 1)
            pool.wait_ge(bc_in, 16)
            pool.wait_ge(coef_step, COEF_N)
            for i, (cc, bb) in enumerate(((10, 0), (11, 1), (10, 1), (11, 0))):
                pool.tensor_tensor(bprod[:, i, :, :], bcr[:, bb, :, :],
                                   coef[:, cc, :].unsqueeze(2).to_broadcast([128, PAIRS, 16]),
                                   ALU.mult).then_inc(b_prod, 1)

            def table_turns(h):
                n = 5 * h
                if h >= 1:
                    pool.wait_ge(tab_trig, 3 * h)
                for j in range(2):
                    f = st[:, 1, 2 * h + j:2 * h + j + 1]
                    pool.tensor_scalar(turn[:, j, :], tv, f, 0.0, ALU.mult, ALU.add).then_inc(tab_work, 1)
                pool.wait_ge(tab_work, n + 2)
                pool.tensor_scalar(whole[:, :, :], turn[:, :, :], 1.0, MAGIC, ALU.mult, ALU.add).then_inc(tab_work, 1)
                pool.wait_ge(tab_work, n + 3)
                pool.tensor_scalar(whole[:, :, :], whole[:, :, :], -MAGIC, 1.0, ALU.add, ALU.mult).then_inc(tab_work, 1)
                pool.wait_ge(tab_work, n + 4)
                pool.tensor_tensor(turn[:, :, :], turn[:, :, :], whole[:, :, :], ALU.subtract).then_inc(tab_work, 1)

            def back_products(k):
                pool.wait_ge(ssm_scan, 2 * k + 2)
                if k == 0:
                    pool.wait_ge(bias_out, 16)
                    pool.wait_ge(bias_mm, 2)
                if k >= 2:
                    pool.wait_ge(ssm_state, 2 * (k - 1))
                cs = CS[(k // 2) % 2]
                for i in range(2):
                    pool.tensor_tensor(N[k % 2][:, i, :, :], Z[k % 2][:, :, :],
                                       cs[:, i, k % 2, :].unsqueeze(1).to_broadcast([128, 2, 256]),
                                       ALU.mult).then_inc(ssm_back, 1)

            for step, i in STEPS:
                if step == "tab":
                    table_turns(i)
                elif step == "back":
                    back_products(i)
                elif step == "c_blocks":
                    pool.wait_ge(h_tr, KT // 2)
                    pool.memset(vblk[:, :, :], 0.0).then_inc(cmp_zeroed, 1)
                    pool.memset(pcmp[:, :, :], 0.0).then_inc(cmp_zeroed, 1)
                elif step == "z":
                    for j in range(4):
                        pool.wait_ge(z_hi, j + 1)
                        pool.tensor_tensor(ZL[:, 2 * j:2 * j + 2, :], uT[:, 2 * j:2 * j + 2, :],
                                           ZH[:, 2 * j:2 * j + 2, :].bitcast(fp32), ALU.subtract).then_inc(z_lo, 1)
                elif step == "pv":
                    h = i
                    for a in range(2):
                        pool.wait_ge(o_scaled, h + 1)
                        if a:
                            pool.wait_ge(y_added, 2 * h + 1)
                        y = ynsa[:, :, h * HD:(h + 1) * HD]
                        if h == 0 and a == 0:
                            pool.wait_ge(cmp_o_out, 4)
                        pool.tensor_tensor(y, y, T[h % 2][:, a, :, :], ALU.add).then_inc(y_added, 1)

        @block.scalar
        def _(act):
            act.dma_start(par[:, :], params).then_inc(par_in, 16)
            act.dma_start(oh[:, :], buckets).then_inc(oh_in, 16)
            act.dma_start(bcr[:, :, :, :].rearrange("p a b c -> p (a b c)"), bc).then_inc(bc_in, 16)

            eps_ap = rs[:, 2, 0:1]
            half_pi_ap = rs[:, 2, 1:2]

            def square_sum(junk_, v, part):
                nc.scalar.activation(junk_, v, ACT.Square, accum_out=part).then_inc(ss_ready, 1)

            def load_root(n):
                nc.scalar.activation(spare[:, n:n + 1], eps_ap, ACT.Sqrt).then_inc(root_loaded, 1)

            def root(n):
                act.wait_ge(sum_ready, n + 1)
                nc.scalar.activation(rs[:, 1, :], rs[:, 0, :], ACT.Sqrt, scale=1.0 / D,
                                     bias=eps_ap).then_inc(std_ready, 1)

            def h_transposed(n, gain):
                for kp in range(KT // 2):
                    act.wait_ge(h_tr, 8 * n + kp + 1)
                    for j in range(2):
                        k = 2 * kp + j
                        nc.scalar.activation(AH[:, k, :], TB[kp % 4][:, j * 256:(j + 1) * 256], ACT.Copy,
                                             scale=gain[:, k:k + 1]).then_inc(h_hi, 1)

            def split_hi(s, no, slot_value):
                slot = s % SLOTS
                act.wait_ge(piece_in[slot], slot_value)
                if no >= 2:
                    act.wait_ge(piece_used, used_before(no - 2))
                n = width(s)
                nc.scalar.activation(whi[no % 2][:, 0:n], raw[slot][:, 0:n], ACT.Copy).then_inc(hi_ready, 1)

            split_piece = [s for s in range(N0) if is_split[s]]

            def used_before(no):
                return split_piece[no] + 1

            act.wait_ge(par_in, 16)
            nc.scalar.activation(coef[:, 0, :], P("ldt"), ACT.Exp).then_inc(coef_act, 1)
            act.wait_ge(coef_step, 2)
            nc.scalar.activation(st[:, 0, :], coef[:, 1, :], ACT.Exp).then_inc(coef_act, 1)
            load_root(0)
            act.wait_ge(bias_mm, 1)
            nc.scalar.activation(brow[:, :], G[0][0:HEADS, 0, 0:BIAS_W], ACT.Copy, scale=-1.0).then_inc(bias_row_ready, 1)
            act.wait_ge(bias_row_ready, 1)
            act.dma_start(bass.AP(bias_dram.tensor, 0, [[BIAS_PITCH, HEADS], [BIAS_W + 1, 128], [1, BIAS_W]]),
                          brow[:, :].unsqueeze(1).to_broadcast([HEADS, 128, BIAS_W])).then_inc(bias_out, 16)
            for j in range(2):
                act.wait_ge(x_in[2 * j], 16)
                if j:
                    act.wait_ge(ss_ready, 1)
                square_sum(junk[0][:, :], X[:, 0, 1024 * j:1024 * j + 1024], parts[:, 0, j:j + 1])
            root(0)
            act.wait_ge(bias_mm, 2)
            nc.scalar.activation(biasc[:, :, :, :], G[0][:, 1, :].rearrange("p (t n h) -> p t h n", t=2, n=CMP_PAD),
                                 ACT.Copy, scale=-1.0).then_inc(biasc_ready, 1)
            h_transposed(0, P("n1"))

            def evac(g):
                b = G[g % 2]
                kind, c = PROD[g]
                s_last = first_piece[(kind, c)] + (0 if kind == "gate" else 3)
                act.wait_ge(piece_used, s_last + 1)
                if kind == "gate":
                    nc.scalar.activation(gates[:, :, :], b[:, :, 0:48], ACT.Sigmoid).then_inc(gate_ready, 1)
                elif c < 2:
                    for j in range(2):
                        nc.scalar.activation(uT[:, 4 * c + 2 * j:4 * c + 2 * j + 2, :],
                                             b[:, j, :].rearrange("p (m t) -> p m t", m=2), ACT.Copy
                                             ).then_inc(u_ready, 1)
                elif c in (3, 4):
                    for j in range(2):
                        m = 4 * (c - 3) + 2 * j
                        nc.scalar.activation(qT[:, m:m + 2, :], b[:, j, :].rearrange("p (m t) -> p m t", m=2),
                                             ACT.Copy, scale=-(HD ** -0.5)).then_inc(q_ready, 1)
                elif c == 2:
                    compress_layout(act_copy, b, 0)
                else:
                    key_layout(act_copy, b, c - 5, 0)
                    nc.scalar.activation(vrow[c - 5][:, :, :], b[:, 1, :].rearrange("p (t n) -> p t n", t=2),
                                         ACT.Copy).then_inc(kv_ready, 1)

            def act_copy(dst, src, signal):
                nc.scalar.activation(dst, src, ACT.Copy).then_inc(signal, 1)

            def table_trig(h):
                act.wait_ge(tab_work, 5 * h + 5)
                if h >= 2:
                    act.wait_ge(ssm_back, 4 * (h - 1))
                cs = CS[h % 2]
                nc.scalar.activation(cs[:, 1, :, :], turn[:, :, :], ACT.Sin, scale=TWO_PI_DOWN).then_inc(tab_trig, 1)
                nc.scalar.activation(whole[:, :, :], turn[:, :, :], ACT.Abs).then_inc(tab_trig, 1)
                act.wait_ge(tab_trig, 3 * h + 2)
                nc.scalar.activation(cs[:, 0, :, :], whole[:, :, :], ACT.Sin, scale=-TWO_PI_DOWN,
                                     bias=half_pi_ap).then_inc(tab_trig, 1)

            for step, i in STEPS:
                if step == "split":
                    if is_split[i]:
                        split_hi(i, split_no[i], 16 * (i // SLOTS + 1))
                elif step == "evac":
                    evac(i)
                elif step == "trig":
                    table_trig(i)
                elif step == "coef_trig":
                    nc.scalar.activation(coef[:, 4, :], st[:, 1, :], ACT.Sin, scale=TWO_PI_DOWN).then_inc(coef_act, 1)
                    nc.scalar.activation(coef[:, 2, :], st[:, 1, :], ACT.Abs).then_inc(coef_act, 1)
                    act.wait_ge(coef_act, 4)
                    nc.scalar.activation(coef[:, 5, :], coef[:, 2, :], ACT.Sin, scale=-TWO_PI_DOWN,
                                         bias=half_pi_ap).then_inc(coef_act, 1)
                elif step == "b_T":
                    for r in range(2):
                        for j in range(2):
                            act.wait_ge(b_T, 2 * r + j + 1)
                            nc.scalar.activation(BL[:, 4 * j:4 * j + 4, r, :],
                                                 BU[j][:, :, :].rearrange("p a (b n) -> p (a b) n", b=2),
                                                 ACT.Copy).then_inc(b_T_out, 1)
                elif step == "hidden":
                    act.wait_ge(piece_used, first_piece[("cmp", 1)] + 2)
                    nc.scalar.activation(hrow[:, :], hid_ps, ACT.Gelu_apprx_tanh).then_inc(hrow_ready, 1)
                elif step == "hid_T_out":
                    act.wait_ge(hid_T, 1)
                    act.wait_ge(zeroed, 3)
                    act.wait_ge(hidv_zero, 1)
                    src = OB[:, 0:128].rearrange("p (j v n) -> p j v n", j=2, v=KV)
                    nc.scalar.activation(hidk[:, :, :, 0:CMP_PAD].rearrange("p j v n -> p (j v) n"),
                                         src.rearrange("p j v n -> p (j v) n"), ACT.Copy).then_inc(hid_ready, 1)
                    for j in range(2):
                        src = OB[:, 128 + 64 * j:192 + 64 * j].rearrange("p (v n) -> p v n", v=KV)
                        nc.scalar.activation(hidv[:, j, :, :, 0:CMP_PAD],
                                             src.unsqueeze(2).to_broadcast([128, KV, 4, CMP_PAD]),
                                             ACT.Copy).then_inc(hid_ready, 1)
                elif step == "cmp_kv_out":
                    act.wait_ge(cmp_kv, 2)
                    nc.scalar.activation(kcmp[:, :, :], kc_ps.rearrange("p (v n) -> p v n", v=KV),
                                         ACT.Copy).then_inc(cmp_kv_out, 1)
                elif step == "cmp_exp":
                    act.wait_ge(cmp_step, 4)
                    nc.scalar.activation(lcmp, lcmp, ACT.Exp, scale=-1.0).then_inc(cmp_exp, 1)
                elif step == "cmp_T_out":
                    act.wait_ge(cmp_T, 1)
                    for t in range(TILES):
                        nc.scalar.activation(pcT[:, 4 * t:4 * t + 4, :], G[0][:, t, :].rearrange("p (k q) -> p k q", q=128),
                                             ACT.Copy).then_inc(cmp_T_out, 1)
                elif step == "cmp_o_out":
                    act.wait_ge(cmp_o, i + 1)
                    nc.scalar.activation(ynsa[:, i // 2, 512 * (i % 2):512 * (i % 2) + 512], CMP_O[i],
                                         ACT.Copy).then_inc(cmp_o_out, 1)
                elif step == "gelu":
                    act.wait_ge(y_out, 2 * i + 2)
                    v = uT[:, 2 * i:2 * i + 2, :]
                    nc.scalar.activation(v, v, ACT.Gelu_apprx_tanh).then_inc(z_ready, 1)
                elif step == "z":
                    for j in range(4):
                        act.wait_ge(z_ready, 4)
                        nc.scalar.activation(ZH[:, 2 * j:2 * j + 2, :], uT[:, 2 * j:2 * j + 2, :], ACT.Copy).then_inc(z_hi, 1)
                elif step == "glu_gate":
                    c = i
                    act.wait_ge(piece_used, G0 + 2 * c + 2)
                    for m in range(4):
                        n = 4 * c + m
                        nc.scalar.activation(mixv[c][:, m, :], G[1][:, m // 2, (m % 2) * 256:(m % 2 + 1) * 256],
                                             ACT.Sigmoid, bias=P("bglu")[:, n:n + 1]).then_inc(sg_ready, 1)
                elif step == "glu_mix":
                    c = i
                    act.wait_ge(mix_ready, c + 1)
                    nc.scalar.activation(AH[:, 4 * c:4 * c + 4, :], mixv[c][:, :, :], ACT.Copy).then_inc(mix_hi, 1)
                elif step == "yT":
                    act.wait_ge(yt_done, i + 1)
                    nc.scalar.activation(AH[:, 8 + i, :], YB[:, 0:256], ACT.Copy).then_inc(yt_hi, 1)
                elif step == "add":
                    for t in range(TILES):
                        act.wait_ge(x_added, 2 * i + t + 1)
                        act.wait_ge(ss_ready, 2 + 2 * i + t)
                        square_sum(junk[0][:, 0:512], X[:, t, 512 * i:512 * i + 512], parts[:, t, i:i + 1])
                elif step == "qk":
                    h = i
                    for a in range(2):
                        for t in (1, 0):
                            j = 4 * h + 2 * a + (1 - t)
                            act.wait_ge(lg_ready, j + 1)
                            if h >= 2 and a == 0 and t == 1:
                                act.wait_ge(pT_done, 2 * (h - 1))
                                act.wait_ge(al_step, 2 * (h - 1))
                            cols = slice(0, 256) if t else slice(256, 384)
                            nc.scalar.activation(prob[h % 2][:, a, cols], lg[h % 2][:, a, cols], ACT.Exp, scale=-1.0,
                                                 bias=nmax[h % 2][:, 2 * a + t:2 * a + t + 1],
                                                 accum_out=esum[h % 2][:, 2 * a + t:2 * a + t + 1]
                                                 ).then_inc(exp_ready, 1)
                elif step == "pT":
                    act.wait_ge(pT_done, 2 * i + 1)
                    if i >= 2:
                        act.wait_ge(pv_done, i - 1)
                    nc.scalar.activation(pT[i % 2][:, 0, :], TB[0][:, 0:384], ACT.Copy).then_inc(pT_out, 1)

            load_root(1)
            root(1)
            h_transposed(1, P("n2"))

            def mlp_split(i, base, j, per):
                s = base + j
                no = SP0 + (base - N0) + j
                slot = s % SLOTS
                act.wait_ge(piece_in[slot], i * (4 * per) + 16 * (s // SLOTS + 1))
                act.wait_ge(piece_used, i * per + (s - 1))
                nc.scalar.activation(whi[no % 2][:, :], raw[slot][:, :], ACT.Copy).then_inc(hi_ready, 1)

            def last_sums(c):
                for t in range(TILES):
                    act.wait_ge(x_added, 16 + 2 * c + t + 1)
                    act.wait_ge(ss_ready, 10 + 2 * c + t)
                    square_sum(junk_mlp[:, :], X[:, t, 512 * c:512 * c + 512], parts[:, t, c:c + 1])

            def relu(i, f, c, per):
                act.wait_ge(piece_used, i * (4 * per) + (N0 + 64 * f + 4 * c + 4))
                if f or c > 0:
                    act.wait_ge(sq_ready, i * per + max(8 * f + c - 1, 1))
                nc.scalar.activation(RT[c % 2][:, :, :].rearrange("p m t -> p (m t)"),
                                     G[c % 2][:, :, :].rearrange("p a n -> p (a n)"),
                                     ACT.Relu).then_inc(relu_ready, 1)

            def squared_hi(i, f, c, per, dst):
                act.wait_ge(sq_ready, i * per + (8 * f + c + 1))
                if f and isinstance(i, int) and c == 0:
                    act.wait_ge(piece_used, N0 + 64)
                nc.scalar.activation(dst, SQ[c % 2][:, :, :], ACT.Copy).then_inc(mlp_hi, 1)

            for f in range(2):
                up0 = N0 + 64 * f
                for j in range(8):
                    mlp_split(0, up0, j, 0)
                    if j == 4:
                        nc_relu = relu(0, f, 0, 0)
                    if j == 5:
                        squared_hi(0, f, 0, 0, MH[:, 0:4, :])
                with act.Fori(0, 3) as i:
                    for j in range(8):
                        mlp_split(i, up0 + 8, j, 8)
                        if j == 0:
                            relu(i, f, 1, 2)
                        if j == 1:
                            squared_hi(i, f, 1, 2, MH[:, bass.ds(i * 8 + 4, 4), :])
                        if j == 4:
                            relu(i, f, 2, 2)
                        if j == 5:
                            squared_hi(i, f, 2, 2, MH[:, bass.ds(i * 8 + 8, 4), :])
                dn0 = up0 + 32
                mlp_split(0, dn0, 0, 0)
                relu(0, f, 7, 0)
                squared_hi(0, f, 7, 0, MH[:, 28:32, :])
                for j in range(1, 8):
                    mlp_split(0, dn0, j, 0)
                if f == 0:
                    with act.Fori(0, 3) as i:
                        for j in range(8):
                            mlp_split(i, dn0 + 8, j, 8)
                else:
                    for c in range(1, 4):
                        for j in range(8):
                            mlp_split(0, dn0 + 8 * c, j, 0)
                            if j == 1:
                                last_sums(c - 1)
            load_root(2)
            last_sums(3)
            root(2)
            act.wait_ge(rinv_ready, 3)
            act.wait_ge(gained, 8)
            for j in range(2):
                v = X[:, 0, 1024 * j:1024 * j + 1024]
                nc.scalar.activation(v, v, ACT.Copy, scale=rs[:, 1, 0:1]).then_inc(fin_step, 1)

        @block.vector
        def _(dve):
            V = nc.vector
            V.memset(rs[:, 2, 0:1], EPS).then_inc(coef_step, 1)
            V.memset(rs[:, 2, 1:2], math.pi / 2).then_inc(zeroed, 1)
            n = [1]

            def link(ins):
                n[0] += 1
                ins.then_inc(coef_step, 1)
                dve.wait_ge(coef_step, n[0])

            c = coef
            dve.wait_ge(par_in, 16)
            dve.wait_ge(coef_act, 1)
            link(V.tensor_tensor(c[:, 1, :], c[:, 0, :], P("are"), ALU.mult))
            link(V.tensor_tensor(c[:, 3, :], c[:, 0, :], P("aim"), ALU.mult))
            link(V.tensor_scalar(c[:, 6, :], c[:, 3, :], INV_2PI, MAGIC, ALU.mult, ALU.add))
            link(V.tensor_scalar(c[:, 6, :], c[:, 6, :], -MAGIC, None, ALU.add))
            link(V.scalar_tensor_tensor(out=c[:, 7, :], in0=c[:, 6, :], scalar=-C1, in1=c[:, 3, :],
                                        op0=ALU.mult, op1=ALU.add))
            link(V.scalar_tensor_tensor(out=c[:, 8, :], in0=c[:, 6, :], scalar=-C2, in1=c[:, 7, :],
                                        op0=ALU.mult, op1=ALU.add))
            link(V.scalar_tensor_tensor(out=c[:, 7, :], in0=c[:, 6, :], scalar=-C3, in1=c[:, 8, :],
                                        op0=ALU.mult, op1=ALU.add))
            link(V.tensor_scalar(c[:, 8, :], c[:, 7, :], INV_2PI, 0.5, ALU.mult, ALU.min))
            link(V.tensor_scalar(st[:, 1, :], c[:, 8, :], -0.5, None, ALU.max))

            def row_scales(k, n_parts):
                V.tensor_reduce(out=rs[:, 0, :], in_=parts[:, :, 0:n_parts], axis=AX.X, op=ALU.add).then_inc(sum_ready, 1)
                dve.wait_ge(std_ready, k + 1)
                V.reciprocal(rs[:, 1, :], rs[:, 1, :]).then_inc(rinv_ready, 1)
                dve.wait_ge(rinv_ready, k + 1)
                if k < 2:
                    for t in range(TILES):
                        V.tensor_scalar(diag[:, t, :], ident, rs[:, 1, t:t + 1], None, ALU.mult).then_inc(diag_ready, 1)

            def h_transposed(k, gain):
                for kt in range(KT):
                    kp = kt // 2
                    dve.wait_ge(h_hi, 16 * k + 2 * kp + 2)
                    V.scalar_tensor_tensor(out=AL[:, kt, :], in0=TB[kp % 4][:, (kt % 2) * 256:(kt % 2 + 1) * 256],
                                           scalar=gain[:, kt:kt + 1], in1=AH[:, kt, :].bitcast(fp32), op0=ALU.mult,
                                           op1=ALU.subtract).then_inc(h_lo, 1)

            for j in range(2):
                dve.wait_ge(x_in[2 * j + 1], 16)
                v = X[:, 1, 1024 * j:1024 * j + 1024]
                V.tensor_tensor_reduce(out=junk[1][:, :], in0=v, in1=v, scale=1.0, scalar=0.0,
                                       op0=ALU.mult, op1=ALU.add, accum_out=parts[:, 1, j:j + 1]).then_inc(own_sums, 1)
                dve.wait_ge(own_sums, j + 1)
            dve.wait_ge(ss_ready, 2)
            row_scales(0, 2)
            h_transposed(0, P("n1"))

            def coefficients():
                dve.wait_ge(coef_act, 5)
                link(V.tensor_tensor(c[:, 2, :], st[:, 0, :], c[:, 4, :], ALU.mult))
                link(V.tensor_tensor(c[:, 5, :], st[:, 0, :], c[:, 5, :], ALU.mult))
                link(V.tensor_scalar(c[:, 5, :], c[:, 5, :], -1.0, None, ALU.add))
                link(V.tensor_tensor(c[:, 6, :], P("are"), P("are"), ALU.mult))
                link(V.tensor_tensor(c[:, 7, :], P("aim"), P("aim"), ALU.mult))
                link(V.tensor_tensor(c[:, 6, :], c[:, 6, :], c[:, 7, :], ALU.add))
                link(V.reciprocal(c[:, 6, :], c[:, 6, :]))
                link(V.tensor_tensor(c[:, 7, :], c[:, 5, :], P("are"), ALU.mult))
                link(V.tensor_tensor(c[:, 8, :], c[:, 2, :], P("aim"), ALU.mult))
                link(V.tensor_tensor(c[:, 7, :], c[:, 7, :], c[:, 8, :], ALU.add))
                link(V.tensor_tensor(c[:, 10, :], c[:, 7, :], c[:, 6, :], ALU.mult))
                link(V.tensor_tensor(c[:, 7, :], c[:, 2, :], P("are"), ALU.mult))
                link(V.tensor_tensor(c[:, 8, :], c[:, 5, :], P("aim"), ALU.mult))
                link(V.tensor_tensor(c[:, 7, :], c[:, 7, :], c[:, 8, :], ALU.subtract))
                link(V.tensor_tensor(c[:, 11, :], c[:, 7, :], c[:, 6, :], ALU.mult))
                assert n[0] == COEF_N

            def c_in_blocks():
                dve.wait_ge(zeroed, 4)
                dve.wait_ge(bc_in, 16)
                for half in range(2):
                    p = slice(64 * half, 64 * half + 64)
                    w = slice(16 * half, 16 * half + 16)
                    V.tensor_copy(CL[p, 0, :, w], bcr[p, 2, :, :]).then_inc(c_blocks, 1)
                    V.tensor_scalar(CL[p, 1, :, w], bcr[p, 3, :, :], -1.0, None, ALU.mult).then_inc(c_blocks, 1)

            def b_in_blocks():
                dve.wait_ge(b_prod, 4)
                for half in range(2):
                    p = slice(64 * half, 64 * half + 64)
                    w = slice(16 * half, 16 * half + 16)
                    V.tensor_tensor(BD[p, 0, :, w], bprod[p, 0, :, :], bprod[p, 1, :, :], ALU.subtract).then_inc(b_blocks, 1)
                    V.tensor_tensor(BD[p, 1, :, w], bprod[p, 2, :, :], bprod[p, 3, :, :], ALU.add).then_inc(b_blocks, 1)

            def split_lo(s, no):
                dve.wait_ge(hi_ready, no + 1)
                n = width(s)
                V.tensor_tensor(wlo[s % SLOTS][:, 0:n], raw[s % SLOTS][:, 0:n], whi[no % 2][:, 0:n].bitcast(fp32),
                                ALU.subtract).then_inc(lo_ready, 1)

            def rotate_and_scan(k):
                cs = CS[(k // 2) % 2]
                r = st[:, 0, k:k + 1].to_broadcast([128, 256])
                dve.wait_ge(bu_done, k + 1)
                dve.wait_ge(tab_trig, 3 * (k // 2 + 1))
                if k >= 1:
                    dve.wait_ge(ssm_rot, 2 * k)
                for i in range(2):
                    V.tensor_tensor(M[:, i, :, :], BU[k % 2][:, :, :],
                                    cs[:, i, k % 2, :].unsqueeze(1).to_broadcast([128, 2, 256]),
                                    ALU.mult).then_inc(ssm_prod, 1)
                dve.wait_ge(ssm_prod, 2 * k + 2)
                if k >= 1:
                    dve.wait_ge(ssm_scan, 2 * k)
                V.tensor_tensor(W[:, 0, :], M[:, 0, 0, :], M[:, 1, 1, :], ALU.add).then_inc(ssm_rot, 1)
                V.tensor_tensor(W[:, 1, :], M[:, 0, 1, :], M[:, 1, 0, :], ALU.subtract).then_inc(ssm_rot, 1)
                if k >= 2:
                    dve.wait_ge(ssm_back, 2 * (k - 1))
                for i in range(2):
                    dve.wait_ge(ssm_rot, 2 * k + i + 1)
                    V.tensor_tensor_scan(Z[k % 2][:, i, :], r, W[:, i, :], 0.0, ALU.mult, ALU.add).then_inc(ssm_scan, 1)

            def turned_states(k):
                dve.wait_ge(ssm_back, 2 * k + 2)
                if k >= 2:
                    dve.wait_ge(y_done, k - 1)
                b = N[k % 2]
                V.tensor_tensor(S[k % 2][:, 0, :], b[:, 0, 0, :], b[:, 1, 1, :], ALU.subtract).then_inc(ssm_state, 1)
                V.tensor_tensor(S[k % 2][:, 1, :], b[:, 0, 1, :], b[:, 1, 0, :], ALU.add).then_inc(ssm_state, 1)

            def octet_out(q):
                dve.wait_ge(y_done, 4 * q + 4)
                V.scalar_tensor_tensor(out=uT[:, q, :], in0=uT[:, q, :], scalar=P("d")[:, q:q + 1],
                                       in1=YB[:, (q % 2) * 256:(q % 2 + 1) * 256], op0=ALU.mult,
                                       op1=ALU.add).then_inc(y_out, 1)

            def dve_copy(dst, src, signal):
                V.tensor_copy(dst, src).then_inc(signal, 1)

            CM = [0]

            def cmp_link(ins):
                CM[0] += 1
                ins.then_inc(cmp_step, 1)
                dve.wait_ge(cmp_step, CM[0])

            TH = TILES * HEADS
            for step, i in STEPS:
                if step == "split":
                    if is_split[i]:
                        split_lo(i, split_no[i])
                elif step == "evac":
                    kind, cc = PROD[i]
                    if kind == "in" and cc in (2, 5, 6):
                        dve.wait_ge(piece_used, first_piece[(kind, cc)] + 4)
                        if cc == 2:
                            compress_layout(dve_copy, G[i % 2], 1)
                        else:
                            key_layout(dve_copy, G[i % 2], cc - 5, 1)
                elif step == "coef":
                    coefficients()
                elif step == "c_blocks":
                    c_in_blocks()
                elif step == "b_blocks":
                    b_in_blocks()
                elif step == "flat":
                    dve.wait_ge(kc_ready, 4)
                    dve.wait_ge(pads, 1)
                    for kind in range(2):
                        v = kcat[:, 512 * kind:512 * kind + 16]
                        win = bass.AP(v.tensor, v.offset, [list(v.ap[0]), [1, KT], [8, 64]])
                        V.tensor_tensor(flat[:, kind, :, :], win, P("pek" if kind == 0 else "pev").unsqueeze(2)
                                        .to_broadcast([128, KT, 64]), ALU.add).then_inc(flat_ready, 1)
                elif step == "rot":
                    rotate_and_scan(i)
                elif step == "state":
                    turned_states(i)
                elif step == "y":
                    if i % 4 == 3:
                        octet_out(i // 4)
                elif step == "cmp_kv_out":
                    dve.wait_ge(cmp_zeroed, 2)
                    dve.wait_ge(cmp_kv_out, 1)
                    for r in range(4):
                        p = slice(32 * r, 32 * r + 32)
                        V.tensor_copy(vblk[p, :, HD * r:HD * r + HD], vc_ps[p, :, :]).then_inc(cmp_kv_out, 1)
                elif step == "cmp_l_out":
                    dve.wait_ge(cmp_logits, i + 1)
                    cmp_link(V.tensor_tensor(lcmp[:, i::2, :], OB[:, 0:256].rearrange("p (k n) -> p k n", n=CMP_PAD),
                                             lcmp[:, i::2, :], ALU.add))
                elif step == "cmp_min":
                    cmp_link(V.tensor_reduce(out=cst[:, 0, :], in_=lcmp, axis=AX.X, op=ALU.min))
                    cmp_link(V.tensor_tensor(lcmp, lcmp, cst[:, 0, :].unsqueeze(2).to_broadcast([128, TH, CMP_PAD]),
                                             ALU.subtract))
                elif step == "cmp_p":
                    dve.wait_ge(cmp_exp, 1)
                    cmp_link(V.tensor_reduce(out=cst[:, 1, :], in_=lcmp, axis=AX.X, op=ALU.add))
                    cmp_link(V.reciprocal(cst[:, 2, :], cst[:, 1, :]))
                    dve.wait_ge(gate_ready, 1)
                    for t in range(TILES):
                        cmp_link(V.scalar_tensor_tensor(
                            out=cst[:, 3, t * HEADS:(t + 1) * HEADS], in0=cst[:, 2, t * HEADS:(t + 1) * HEADS],
                            scalar=P("valid")[:, t:t + 1],
                            in1=gates[:, t, :].rearrange("p (h i) -> p h i", i=3)[:, :, 0],
                            op0=ALU.mult, op1=ALU.mult))
                    cmp_link(V.tensor_tensor(pcmp[:, :, 0:CMP_PAD], lcmp,
                                             cst[:, 3, :].unsqueeze(2).to_broadcast([128, TH, CMP_PAD]), ALU.mult))
                elif step == "qk":
                    h = i
                    dve.wait_ge(qk_done, h + 1)
                    if h == 0:
                        dve.wait_ge(bias_in, 16)
                    if h >= 2:
                        dve.wait_ge(exp_ready, 4 * (h - 1))
                    for a in range(2):
                        for t in (1, 0):
                            cols = slice(0, 256) if t else slice(256, 384)
                            b = bias[:, h, :] if t else bias[:, h, 128:256]
                            V.tensor_tensor_reduce(out=lg[h % 2][:, a, cols], in0=G[0][:, a, cols], in1=b, scale=1.0,
                                                   scalar=3.0e38, op0=ALU.add, op1=ALU.min,
                                                   accum_out=nmax[h % 2][:, 2 * a + t:2 * a + t + 1]
                                                   ).then_inc(lg_ready, 1)
                elif step == "pT":
                    h = i
                    dve.wait_ge(exp_ready, 4 * h + 4)
                    if h >= 2:
                        dve.wait_ge(o_scaled, h - 1)
                    V.reciprocal(alpha[h % 2][:, 0, :], esum[h % 2][:, :]).then_inc(al_step, 1)
                    dve.wait_ge(pT_done, 2 * h + 2)
                    if h >= 2:
                        dve.wait_ge(pv_done, h - 1)
                    V.tensor_copy(pT[h % 2][:, 1, :], TB[1][:, 0:384]).then_inc(pT_out, 1)
                    dve.wait_ge(al_step, 2 * h + 1)
                    gv = gates[:, :, 3 * h + 1:3 * h + 3].rearrange("p t a -> p a t")
                    V.tensor_tensor(alpha[h % 2][:, 1, :].rearrange("p (a t) -> p a t", a=2),
                                    alpha[h % 2][:, 0, :].rearrange("p (a t) -> p a t", a=2), gv,
                                    ALU.mult).then_inc(al_step, 1)
                elif step == "glu_gate":
                    dve.wait_ge(sg_ready, 4 * i + 4)
                    V.tensor_tensor(mixv[i][:, :, :], mixv[i][:, :, :], uT[:, 4 * i:4 * i + 4, :],
                                    ALU.mult).then_inc(mix_ready, 1)
                elif step == "glu_mix":
                    dve.wait_ge(mix_hi, i + 1)
                    V.tensor_tensor(AL[:, 4 * i:4 * i + 4, :], mixv[i][:, :, :],
                                    AH[:, 4 * i:4 * i + 4, :].bitcast(fp32), ALU.subtract).then_inc(mix_lo, 1)
                elif step == "yT":
                    dve.wait_ge(yt_hi, i + 1)
                    V.tensor_tensor(AL[:, 8 + i, :], YB[:, 0:256], AH[:, 8 + i, :].bitcast(fp32),
                                    ALU.subtract).then_inc(yt_lo, 1)
                elif step == "add":
                    dve.wait_ge(piece_used, O0 + 4 * i + 4)
                    if i == 0:
                        for q in range(4):
                            dve.wait_ge(x_in[q], 32)
                    for t in range(TILES):
                        v = X[:, t, 512 * i:512 * i + 512]
                        V.tensor_tensor(v, v, G[(i + 1) % 2][:, t, :], ALU.add).then_inc(x_added, 1)
                elif step == "pv":
                    h = i
                    dve.wait_ge(pv_done, h + 1)
                    dve.wait_ge(al_step, 2 * h + 2)
                    if h >= 2:
                        dve.wait_ge(y_added, 2 * (h - 1))
                    V.tensor_tensor(T[h % 2][:, :, :, :].rearrange("p a t d -> p (a t) d"),
                                    o_ps[:, :, :, :].rearrange("p a t d -> p (a t) d"),
                                    alpha[h % 2][:, 1, :].unsqueeze(2).to_broadcast([128, 4, HD]),
                                    ALU.mult).then_inc(o_scaled, 1)

            dve.wait_ge(ss_ready, 2 + 8)
            row_scales(1, 4)
            h_transposed(1, P("n2"))

            def mlp_split(i, base, j, per):
                no = SP0 + (base - N0) + j
                dve.wait_ge(hi_ready, i * per + (no + 1))
                slot = (base + j) % SLOTS
                V.tensor_tensor(wlo[slot][:, :], raw[slot][:, :], whi[no % 2][:, :].bitcast(fp32),
                                ALU.subtract).then_inc(lo_ready, 1)

            def square(i, f, cc, per):
                dve.wait_ge(relu_ready, i * per + (8 * f + cc + 1))
                if f or cc > 0:
                    dve.wait_ge(mlp_lo, i * per + max(8 * f + cc - 1, 1))
                V.tensor_tensor(SQ[cc % 2][:, :, :], RT[cc % 2][:, :, :], RT[cc % 2][:, :, :],
                                ALU.mult).then_inc(sq_ready, 1)

            def squared_lo(i, f, cc, per, dst, hi):
                dve.wait_ge(mlp_hi, i * per + (8 * f + cc + 1))
                V.tensor_tensor(dst, SQ[cc % 2][:, :, :], hi.bitcast(fp32), ALU.subtract).then_inc(mlp_lo, 1)

            def down_rows(i, f, cc, per, cols):
                dve.wait_ge(piece_used, i * (8 * per) + (N0 + 64 * f + 32 + 8 * cc + 8))
                bank = G[cc % 2]
                for t in range(TILES):
                    v = X[:, t, cols]
                    V.tensor_tensor(v, v, bank[:, t, :], ALU.add).then_inc(x_added, 1)

            def gain_rows(cc):
                dve.wait_ge(nf_in, 16)
                for t in range(TILES):
                    dve.wait_ge(ss_ready, 10 + 2 * cc + t + 1)
                    v = X[:, t, 512 * cc:512 * cc + 512]
                    V.tensor_tensor(v, v, NF[:, 512 * cc:512 * cc + 512], ALU.mult).then_inc(gained, 1)

            for f in range(2):
                up0 = N0 + 64 * f
                for j in range(8):
                    mlp_split(0, up0, j, 0)
                    if j == 0 and f == 1:
                        down_rows(0, 0, 3, 0, slice(1536, 2048))
                    if j == 4:
                        square(0, f, 0, 0)
                    if j == 5:
                        squared_lo(0, f, 0, 0, ML[:, 0:4, :], MH[:, 0:4, :])
                with dve.Fori(0, 3) as i:
                    for j in range(8):
                        mlp_split(i, up0 + 8, j, 8)
                        if j == 0:
                            square(i, f, 1, 2)
                        if j == 1:
                            squared_lo(i, f, 1, 2, ML[:, bass.ds(i * 8 + 4, 4), :], MH[:, bass.ds(i * 8 + 4, 4), :])
                        if j == 4:
                            square(i, f, 2, 2)
                        if j == 5:
                            squared_lo(i, f, 2, 2, ML[:, bass.ds(i * 8 + 8, 4), :], MH[:, bass.ds(i * 8 + 8, 4), :])
                dn0 = up0 + 32
                mlp_split(0, dn0, 0, 0)
                square(0, f, 7, 0)
                squared_lo(0, f, 7, 0, ML[:, 28:32, :], MH[:, 28:32, :])
                for j in range(1, 8):
                    mlp_split(0, dn0, j, 0)
                for cc in range(1, 4):
                    for j in range(8):
                        mlp_split(0, dn0 + 8 * cc, j, 0)
                        if j == 0:
                            down_rows(0, f, cc - 1, 0, slice(512 * (cc - 1), 512 * cc))
                        if j == 4 and f == 1:
                            gain_rows(cc - 1)
            down_rows(0, 1, 3, 0, slice(1536, 2048))
            dve.wait_ge(ss_ready, 18)
            row_scales(2, 4)
            gain_rows(3)
            dve.wait_ge(fin_step, 2)
            dve.wait_ge(gained, 8)
            for j in range(2):
                v = X[:, 1, 1024 * j:1024 * j + 1024]
                V.tensor_scalar(v, v, rs[:, 1, 1:2], None, ALU.mult).then_inc(fin_step, 1)

        @block.tensor
        def _(pe):
            T_ = nc.tensor

            def mm(o_, l, r, start, stop):
                return T_.matmul(o_, l, r, start=start, stop=stop, skip_group_check=True)

            def three(o_, wh, wl, ah, al, start, stop, stationary):
                if stationary:
                    mm(o_, wh, ah, start, False)
                    mm(o_, wh, al, False, False)
                    return mm(o_, wl, ah, False, stop)
                mm(o_, ah, wh, start, False)
                mm(o_, ah, wl, False, False)
                return mm(o_, al, wh, False, stop)

            def norm_transposes(n):
                for kp in range(KT // 2):
                    if kp == 0:
                        pe.wait_ge(diag_ready, 2 * n + 2)
                    if kp >= 4:
                        pe.wait_ge(h_lo, 16 * n + 2 * (kp - 3))
                    for j in range(2):
                        for t in range(TILES):
                            k = 2 * kp + j
                            last = mm(TB[kp % 4][:, j * 256 + t * 128:j * 256 + (t + 1) * 128],
                                      X[:, t, k * 128:(k + 1) * 128], diag[:, t, :], True, True)
                    last.then_inc(h_tr, 1)

            pe.wait_ge(oh_in, 16)
            pe.wait_ge(par_in, 16)
            table = oh[:, DIST_W + BIAS_W:]
            mm(G[0][0:HEADS, 0, 0:BIAS_W], table, oh[:, DIST_W:DIST_W + BIAS_W], True, True).then_inc(bias_mm, 1)
            for t in range(TILES):
                for n in range(CMP_PAD):
                    at_ = 512 + 128 * t - 16 * n - 31 if n < N_CMP else 0
                    col = (t * CMP_PAD + n) * HEADS
                    last = mm(G[0][:, 1, col:col + HEADS], oh[:, at_:at_ + 128], table, True, True)
            last.then_inc(bias_mm, 1)

            norm_transposes(0)
            pe.wait_ge(biasc_ready, 1)

            def weights_tiles(s, no, k0, b, tiles, start, stop):
                wh, wl = whi[no % 2], wlo[s % SLOTS]
                for k in range(4):
                    for m in tiles:
                        w = slice(512 * k + 128 * m, 512 * k + 128 * m + 128)
                        last = three(b[:, m // 2, (m % 2) * 256:(m % 2 + 1) * 256], wh[:, w], wl[:, w],
                                     AH[:, k0 + k, :], AL[:, k0 + k, :],
                                     start and k == 0 and m % 2 == 0, stop and k == 3, True)
                return last

            def row_tiles(s, no, ah, al, b, width, start, stop):
                wh, wl = whi[no % 2], wlo[s % SLOTS]
                for k in range(4):
                    for t in range(TILES):
                        w = slice(512 * k, 512 * k + 512) if width == 512 else slice(512 * k + 256, 512 * k + 512)
                        o_ = b[:, t, :] if width == 512 else b[:, 1, t * 256:(t + 1) * 256]
                        first = start and k == 0 and (width == 512 or t == 0)
                        last = three(o_, wh[:, w], wl[:, w], ah(k)[:, t * 128:(t + 1) * 128],
                                     al(k)[:, t * 128:(t + 1) * 128], first, stop and k == 3, False)
                return last

            for step, i in STEPS:
                if step == "product":
                    s = i
                    kind, c, g = STREAM[s]
                    if kind == "cmp":
                        pe.wait_ge(piece_in[s % SLOTS], 16 * (s // SLOTS + 1))
                        pe.wait_ge(flat_ready, c + 1)
                        for k in range(8):
                            kt = 8 * g + k
                            last = mm(hid_ps[:, 256 * c:256 * c + 256], flat[:, c, kt, :],
                                      raw[s % SLOTS][:, 256 * k:256 * k + 256], kt == 0, kt == 15)
                        last.then_inc(piece_used, 1)
                        continue
                    if kind == "glu":
                        no = split_no[s]
                        if s == G0:
                            pe.wait_ge(z_lo, 4)
                        if s == G0 + 2:
                            pe.wait_ge(sg_ready, 4)
                        pe.wait_ge(lo_ready, no + 1)
                        wh, wl = whi[no % 2], wlo[s % SLOTS]
                        for k in range(4):
                            for m in range(4):
                                w = slice(512 * k + 128 * m, 512 * k + 128 * m + 128)
                                last = three(G[1][:, m // 2, (m % 2) * 256:(m % 2 + 1) * 256], wh[:, w], wl[:, w],
                                             ZH[:, 4 * g + k, :], ZL[:, 4 * g + k, :],
                                             g == 0 and k == 0 and m % 2 == 0, g == 1 and k == 3, True)
                        last.then_inc(piece_used, 1)
                        continue
                    if kind == "out":
                        if c == 0 and g == 0:
                            pe.wait_ge(sg_ready, 8)
                            pe.wait_ge(mix_lo, 2)
                        if c == 1 and g == 0:
                            pe.wait_ge(lg_ready, 4 * HEADS)
                        if c >= 2 and g == 0:
                            pe.wait_ge(x_added, 2 * (c - 1))
                        if c == 0 and g >= 2:
                            pe.wait_ge(yt_lo, 4 * (g - 1))
                        pe.wait_ge(lo_ready, split_no[s] + 1)
                        row_tiles(s, split_no[s], lambda k: AH[:, 4 * g + k, :], lambda k: AL[:, 4 * g + k, :],
                                  G[(c + 1) % 2], 512, g == 0, g == 3).then_inc(piece_used, 1)
                        continue
                    g_no = prod_no[(kind, c)]
                    b = G[g_no % 2]
                    if g == 0 and g_no >= 2:
                        pe.wait_ge(*EVAC[g_no - 2])
                    if kind == "gate":
                        pe.wait_ge(lo_ready, split_no[s] + 1)
                        wh, wl = whi[split_no[s] % 2], wlo[s % SLOTS]
                        for t in range(TILES):
                            for k in range(KT):
                                w = slice(48 * k, 48 * k + 48)
                                q = slice(t * 128, (t + 1) * 128)
                                last = three(b[:, t, 0:48], wh[:, w], wl[:, w], AH[:, k, q], AL[:, k, q],
                                             k == 0, k == KT - 1, False)
                        last.then_inc(piece_used, 1)
                        continue
                    pe.wait_ge(lo_ready, split_no[s] + 1)
                    if g_no == 0:
                        pe.wait_ge(h_lo, 4 * g + 4)
                    no = split_no[s]
                    if c in (5, 6):
                        weights_tiles(s, no, 4 * g, b, range(2), g == 0, g == 3)
                        last = row_tiles(s, no, lambda k: AH[:, 4 * g + k, :], lambda k: AL[:, 4 * g + k, :],
                                         b, 256, g == 0, g == 3)
                    else:
                        last = weights_tiles(s, no, 4 * g, b, range(4), g == 0, g == 3)
                    last.then_inc(piece_used, 1)
                elif step == "b_T":
                    pe.wait_ge(b_blocks, 4)
                    for r in range(2):
                        for j in range(2):
                            if r:
                                pe.wait_ge(b_T_out, j + 1)
                            for q in range(4):
                                P0 = 4 * (4 * j + q)
                                last = T_.transpose(BU[j][:, q // 2, (q % 2) * 128:(q % 2 + 1) * 128],
                                                    BD[:, r, P0:P0 + 4, :].rearrange("p a b -> p (a b)"), ident)
                            last.then_inc(b_T, 1)
                elif step == "bu":
                    k, q, r = i, i // 4, i % 4
                    pe.wait_ge(u_ready, q // 2 + 1)
                    if k == 0:
                        pe.wait_ge(b_T_out, 4)
                    if k >= 2:
                        pe.wait_ge(ssm_prod, 2 * (k - 1))
                    p = slice(32 * r, 32 * r + 32)
                    for j in range(2):
                        last = mm(BU[k % 2][:, j, :], BL[p, q, j, :], uT[p, q, :], True, True)
                    last.then_inc(bu_done, 1)
                elif step == "y":
                    k, q, r = i, i // 4, i % 4
                    pe.wait_ge(ssm_state, 2 * k + 2)
                    if k == 0:
                        pe.wait_ge(c_blocks, 4)
                    if r == 0 and q >= 1:
                        pe.wait_ge(y_out, q)
                    o_ = YB[32 * r:32 * r + 32, (q % 2) * 256:(q % 2 + 1) * 256]
                    mm(o_, CL[:, 0, k, :], S[k % 2][:, 0, :], True, False)
                    mm(o_, CL[:, 1, k, :], S[k % 2][:, 1, :], False, True).then_inc(y_done, 1)
                elif step == "cmp_kv":
                    pe.wait_ge(hid_ready, 3)
                    for j in range(2):
                        last = mm(kc_ps, P("w2k")[:, 128 * j:128 * j + 128],
                                  hidk[:, j, :, :].rearrange("p v n -> p (v n)"), j == 0, j == 1)
                    last.then_inc(cmp_kv, 1)
                    for v in range(KV):
                        for j in range(2):
                            hv = hidv[:, j, v, :, :].rearrange("p r n -> p (r n)")
                            last = mm(vc_ps[:, v, :], hv, P("w2v")[:, 64 * j:64 * j + 64], j == 0, j == 1)
                    last.then_inc(cmp_kv, 1)
                elif step == "cmp_l":
                    if i == 0:
                        pe.wait_ge(cmp_kv_out, 5)
                        pe.wait_ge(q_ready, 4)
                    else:
                        pe.wait_ge(cmp_step, 1)
                    for t in range(TILES):
                        for h in range(i, HEADS, 2):
                            p = slice(64 * i, 64 * i + 64)
                            col = (t * HEADS // 2 + h // 2) * CMP_PAD
                            last = mm(OB[:, col:col + CMP_PAD], qT[p, h // 2, t * 128:(t + 1) * 128],
                                      kcmp[p, h // 4, 0:CMP_PAD], True, True)
                    last.then_inc(cmp_logits, 1)
                elif step == "cmp_T":
                    pe.wait_ge(cmp_step, 9)
                    pe.wait_ge(kv_ready, 5)
                    for t in range(TILES):
                        for v in range(KV):
                            k0 = t * HEADS + 4 * v
                            last = T_.transpose(G[0][:, t, v * 128:(v + 1) * 128],
                                                pcmp[:, k0:k0 + 4, :].rearrange("p h n -> p (h n)"), ident)
                    last.then_inc(cmp_T, 1)
                elif step == "cmp_o":
                    pe.wait_ge(cmp_T_out, 2)
                    if i == 3:
                        pe.wait_ge(cmp_o_out, 1)
                    for j in range(2):
                        v = 2 * (i % 2) + j
                        last = mm(CMP_O[i][:, j * 256:(j + 1) * 256], pcT[:, (i // 2) * KV + v, :], vblk[:, v, :], True, True)
                    last.then_inc(cmp_o, 1)
                elif step == "hid_T":
                    pe.wait_ge(hrow_ready, 1)
                    for j in range(4):
                        last = T_.transpose(OB[:, 64 * j:64 * j + 64], hrow[:, 128 * j:128 * j + 128],
                                            ident[0:64, 0:64])
                    last.then_inc(hid_T, 1)
                elif step == "yT":
                    if i == 0:
                        pe.wait_ge(y_out, OCTETS)
                    else:
                        pe.wait_ge(yt_lo, i)
                    pe.wait_ge(y_added, 4 * i + 4)
                    for t in range(TILES):
                        last = T_.transpose(YB[:, t * 128:(t + 1) * 128], ynsa[:, t, i * 128:(i + 1) * 128], ident)
                    last.then_inc(yt_done, 1)
                elif step == "qk":
                    h, v = i, i // 4
                    p = slice(64 * (h % 2), 64 * (h % 2) + 64)
                    if h == 0:
                        pe.wait_ge(kv_ready, 10)
                        pe.wait_ge(cmp_o_out, 4)
                    else:
                        pe.wait_ge(lg_ready, 4 * h)
                    for a in range(2):
                        mm(G[0][:, a, 0:256], qT[p, h // 2, 128:256], kdup[a][p, v, :], True, True)
                        last = mm(G[0][:, a, 256:384], qT[p, h // 2, 0:128], kdup[a][p, v, 0:128], True, True)
                    last.then_inc(qk_done, 1)
                elif step == "pT":
                    h = i
                    if h == 0:
                        pe.wait_ge(ssm_prod, 2 * PAIRS)
                    else:
                        pe.wait_ge(pT_out, 2 * h)
                    for a in range(2):
                        pe.wait_ge(exp_ready, 4 * h + 2 * a + 2)
                        for j in range(3):
                            last = T_.transpose(TB[a][:, j * 128:(j + 1) * 128],
                                                prob[h % 2][:, a, j * 128:(j + 1) * 128], ident)
                        last.then_inc(pT_done, 1)
                elif step == "pv":
                    h, v = i, i // 4
                    pe.wait_ge(pT_out, 2 * h + 2)
                    if h == 0:
                        pe.wait_ge(cmp_o_out, 4)
                    else:
                        pe.wait_ge(o_scaled, h)
                    for a in range(2):
                        vv = vrow[a]
                        cols = slice(v * HD, (v + 1) * HD)
                        mm(o_ps[:, a, 1, :], pT[h % 2][:, a, 0:128], vv[:, 0, cols], True, False)
                        mm(o_ps[:, a, 1, :], pT[h % 2][:, a, 128:256], vv[:, 1, cols], False, True)
                        last = mm(o_ps[:, a, 0, :], pT[h % 2][:, a, 256:384], vv[:, 0, cols], True, True)
                    last.then_inc(pv_done, 1)

            norm_transposes(1)
            for f in range(2):
                up0 = N0 + 64 * f
                sp0 = SP0 + 64 * f

                def up_chunk(i, c, per):
                    for g in range(4):
                        j = 4 * c + g
                        pe.wait_ge(lo_ready, i * (4 * per) + (sp0 + j + 1))
                        if f == 0 and c == 0 and per == 0:
                            pe.wait_ge(h_lo, 16 + 4 * g + 4)
                        weights_tiles(up0 + j, sp0 + j, 4 * g, G[c % 2], range(4), g == 0, g == 3).then_inc(piece_used, 1)

                for c in range(2):
                    if f:
                        pe.wait_ge(x_added, 8 + 8 * f - 2 + 2 * c)
                    up_chunk(0, c, 0)
                with pe.Fori(0, 3) as i:
                    for c in range(2):
                        pe.wait_ge(relu_ready, i * 2 + (8 * f + c + 1))
                        up_chunk(i, 2 + c, 2)

                def down_chunk(i, c, per, last_up):
                    for g in range(8):
                        j = 32 + 8 * c + g
                        pe.wait_ge(lo_ready, i * (8 * per) + (sp0 + j + 1))
                        if last_up and g == 7:
                            pe.wait_ge(mlp_lo, 8 * f + 8)
                        row_tiles(up0 + j, sp0 + j, lambda k: MH[:, 4 * g + k, :], lambda k: ML[:, 4 * g + k, :],
                                  G[c % 2], 512, g == 0, g == 7).then_inc(piece_used, 1)

                for c in range(2):
                    pe.wait_ge(relu_ready, 8 * f + 7 + c)
                    if c == 0:
                        pe.wait_ge(mlp_lo, 8 * f + 7)
                    down_chunk(0, c, 0, c == 0)
                for c in range(2):
                    pe.wait_ge(x_added, 8 + 8 * f + 2 * c + 2)
                    down_chunk(0, 2 + c, 0, False)


COEF_N = 25


def _buckets():
    dist = np.arange(0, SEQ)
    exact = BUCKETS // 2
    large = exact + (np.log(np.maximum(dist, 1).astype(np.float32) / exact)
                     / np.float32(math.log(MAX_DIST / exact)) * (BUCKETS - exact)).astype(np.int32)
    b = np.where(dist < exact, dist, np.minimum(large, BUCKETS - 1))
    hot = np.zeros((BUCKETS + 1, DIST_W + BIAS_W), np.float32)
    for m in range(DIST_W):
        hot[b[m - 512] if m >= 512 else BUCKETS, m] = 1.0
    for j in range(BIAS_W):
        hot[b[255 - j] if j <= 255 else BUCKETS, DIST_W + j] = 1.0
    return hot


def kernel(**inputs):
    import concourse.bacc as bacc
    from concourse.bass_utils import run_bass_kernel_spmd

    a = {k: np.asarray(v) for k, v in inputs.items()}

    def pairs(v):
        v = v.reshape(PAIRS, 2, 64, *v.shape[2:])
        return np.moveaxis(v, 0, 2).reshape(128, PAIRS, *v.shape[3:])

    def columns(v):
        return v.reshape(-1, 128).T

    group, state = a["ssm_a_re"].shape[1:]
    rows = np.arange(128)[:, None]
    parts = {
        "n1": columns(a["norm1_w"][0]), "n2": columns(a["norm2_w"][0]),
        "are": pairs(a["ssm_a_re"][0]), "aim": pairs(a["ssm_a_im"][0]),
        "ldt": pairs(np.broadcast_to(a["ssm_log_dt"][0][:, None], (group, state))),
        "d": columns(a["ssm_d"][0].reshape(-1)), "bglu": columns(a["b_glu"][0]),
        "pek": columns(a["pe_ck"][0].reshape(-1)), "pev": columns(a["pe_cv"][0].reshape(-1)),
        "w2k": np.repeat(a["w_ck2"][0].reshape(2, 128, 1, 64), 2, 2).transpose(1, 0, 2, 3).reshape(128, 256),
        "w2v": a["w_cv2"][0].reshape(2, 128, 64).transpose(1, 0, 2).reshape(128, 128),
        "tv": np.broadcast_to(np.arange(SEQ, dtype=np.float32), (128, SEQ)),
        "ident": np.eye(128, dtype=np.float32),
        "valid": np.concatenate([rows >= 31, rows >= 0], 1).astype(np.float32),
    }
    params = np.concatenate([parts[n] for n in PACK], axis=1)
    bc = np.stack([pairs(a["ssm_b_re"][0]), pairs(a["ssm_b_im"][0]),
                   pairs(a["ssm_c_re"][0].transpose(0, 2, 1)), pairs(a["ssm_c_im"][0].transpose(0, 2, 1))], 1)
    table = np.concatenate([a["rel_table"], np.full((1, HEADS), NEG, np.float32)], 0)
    arrays = {
        "x": a["x"][0], "w_in": a["w_in"][0], "w_glu": a["w_glu"][0], "w_out": a["w_out"][0],
        "w_up": a["w_up"][0], "w_down": a["w_down"][0], "w_ck1": a["w_ck1"][0], "w_cv1": a["w_cv1"][0],
        "nf": a["norm_f_w"], "params": params, "bc": bc.reshape(128, -1),
        "buckets": np.concatenate([_buckets(), table], 1),
    }
    nc = bacc.Bacc("TRN2", target_bir_lowering=False, num_devices=1)
    args, feed = [], {}
    for name, v in arrays.items():
        feed["in_" + name] = np.ascontiguousarray(v)
        args.append(nc.dram_tensor("in_" + name, v.shape, mybir.dt.float32, kind="ExternalInput").ap())
    out = nc.dram_tensor("out_0", (SEQ, D), mybir.dt.float32, kind="ExternalOutput").ap()
    hybrid_layer(nc, *args, out)
    got = run_bass_kernel_spmd(nc, [feed], core_ids=[0])
    return got.results[0]["out_0"].reshape(1, SEQ, D)
```

```python
import math
from contextlib import ExitStack

import numpy as np

import concourse.bass as bass
from concourse import mybir

SEQ, D = 256, 2048
TILES = SEQ // 128
KT = D // 128
HEADS, HD, KV = 16, 64, 4
D_IN = 3632
N_CMP, CMP_PAD = 15, 16
D_FF = 4 * D
FF_HALF = D_FF // 2
PAIRS, OCTETS = 32, 8
BUCKETS, MAX_DIST = 32, 128
EPS = 1e-6
NEG = -1e30
MAGIC = 12582912.0
TWO_PI_DOWN = 6.283185
INV_2PI = 1.0 / (2.0 * math.pi)
C1, C2 = 6.28125, 0.001934051513671875
C3 = 2.0 * math.pi - C1 - C2

PACK = {}
_at = 0
for _n, _w in (("n1", 16), ("n2", 16), ("are", 32), ("aim", 32), ("ldt", 32), ("d", 8), ("bglu", 8),
               ("pek", 16), ("pev", 16), ("w2k", 256), ("w2v", 128), ("tv", 256), ("ident", 128),
               ("valid", 2)):
    PACK[_n] = (_at, _at + _w)
    _at += _w
PACK_W = _at
BIAS_W = 384
DIST_W = 768


def hybrid_layer(nc, x, w_in, w_glu, w_out, w_up, w_down, w_ck1, w_cv1, nf, params, bc, buckets, out):
    fp32, f32r = mybir.dt.float32, mybir.dt.float32r
    ACT, ALU, AX = mybir.ActivationFunctionType, mybir.AluOpType, mybir.AxisListType

    x_v = x.rearrange("(t p) n -> p t n", p=128)
    out_v = out.rearrange("(t p) n -> p t n", p=128)
    BIAS_PITCH = 128 * (BIAS_W + 1)
    bias_dram = nc.dram_tensor("bias_rows", [HEADS, BIAS_PITCH], fp32, kind="Internal").ap()

    IN_CHUNKS = [0, 1, 4, 2, 3, 5, 6]
    STREAM = []

    def four(kind, c):
        STREAM.extend((kind, c, g) for g in range(4))

    for c in range(4):
        four("in", c)
    STREAM.extend(("cmp", c // 2, c % 2) for c in range(4))
    four("in", 4)
    STREAM.append(("gate", 0, 0))
    four("in", 5)
    four("in", 6)
    for c in range(2):
        STREAM.extend(("glu", c, g) for g in range(2))
    OUT_ORDER = [(0, 0), (0, 1), (0, 2), (1, 0), (1, 1), (0, 3), (1, 2), (1, 3)]
    OUT_ORDER += [(2, g) for g in range(4)] + [(3, g) for g in (2, 3, 0, 1)]
    STREAM.extend(("out", c, g) for c, g in OUT_ORDER)
    out_end = [max(i for i, (c, _) in enumerate(OUT_ORDER) if c == cc) for cc in range(4)]
    out_first = [next(g for c, g in OUT_ORDER if c == cc) for cc in range(4)]
    out_last = [[g for c, g in OUT_ORDER if c == cc][-1] for cc in range(4)]
    N0 = len(STREAM)
    is_split = [k != "cmp" for k, _, _ in STREAM]
    split_no = [sum(is_split[:s]) for s in range(N0)]
    SP0 = sum(is_split)
    first_piece = {}
    for _s, (_k, _c, _g) in enumerate(STREAM):
        first_piece.setdefault((_k, _c), _s)
    SLOTS = 4

    def width(s):
        return KT * 48 if STREAM[s][0] == "gate" else 2048


    ctx = ExitStack()
    with ctx:
        BASE = 16512
        K = 1024

        def at(name, shape, dt, off):
            return nc.alloc_sbuf_tensor_at(name, shape, dt, offset=BASE + int(off * K))

        def sem(name):
            return ctx.enter_context(nc.semaphore(name))

        raw = [at(f"raw{i}", [128, 2048], fp32, 8 * i) for i in range(SLOTS)]
        wlo = [at(f"wlo{i}", [128, 2048], f32r, 8 * i) for i in range(SLOTS)]
        whi = [at(f"whi{i}", [128, 2048], f32r, 32 + 8 * i) for i in range(2)]
        AH = at("act_hi", [128, KT, 256], f32r, 48)
        AL = at("act_lo", [128, KT, 256], f32r, 64)
        X = at("x_rows", [128, TILES, D], fp32, 80)
        dg = [at(f"gate_diag{i}", [128, 4, 128], fp32, 116 + 2 * i) for i in range(2)]
        vblk = at("v_cmp_blocks", [128, KV, 256], fp32, 88)
        pcT = at("p_cmp_T", [128, KV, TILES, 128], fp32, 92)
        pcmp = at("p_cmp", [128, TILES * HEADS, 32], fp32, 92)
        prob = [at(f"prob{i}", [128, 2, 384], fp32, 96 + 3 * i) for i in range(2)]
        pT = [at(f"prob_T{i}", [128, 2, 384], fp32, 102 + 3 * i) for i in range(2)]
        lg = [at("logits0", [128, 2, 384], fp32, 108), at("logits1", [128, 2, 384], fp32, 152)]
        BL = at("b_T", [128, OCTETS, 2, 128], fp32, 96)
        CL = at("c_blocks", [128, 2, PAIRS, 32], fp32, 104)
        CS = [at(f"cos_sin{i}", [128, 2, 2, 256], fp32, 112 + 4 * i) for i in range(2)]
        turn = at("turns", [128, 2, 256], fp32, 120)
        whole = at("whole_turns", [128, 2, 256], fp32, 122)
        mixv = [at("mix0", [128, 4, 256], fp32, 120), at("mix1", [128, 4, 256], fp32, 112)]
        uT = at("u_T", [128, OCTETS, 256], fp32, 124)
        qT = at("q_T", [128, 8, 256], fp32, 132)
        junk = [at(f"junk{i}", [128, 1024], fp32, 124 + 4 * i) for i in range(2)]
        kdup = [at(f"k_dup{a}", [128, KV, 256], fp32, 140 + 4 * a) for a in range(2)]
        vrow = [at(f"v_rows{a}", [128, TILES, 256], fp32, 148 + 2 * a) for a in range(2)]
        kcat = at("k_cat", [128, 2 * KV * 128 + 8], fp32, 152)
        hrow = at("hidden_rows", [64, 512], fp32, 152)
        diag = at("row_scales", [128, TILES, 128], fp32, 140)
        flat = at("blocks_flat", [128, 2, KT, 64], fp32, 140)
        hidk = at("hidden_k", [128, 2, KV, 32], fp32, 156.25)
        hidv = at("hidden_v", [128, 2, KV, 4, 32], fp32, 148)
        H2 = [at("h2_hi", [128, 8, 256], f32r, 190), at("h2_lo", [128, 8, 256], f32r, 198)]

        def h2(part, k):
            return H2[part][:, k, :] if k < 8 else (AH, AL)[part][:, k, :]

        o = 157.25

        def small(name, shape):
            nonlocal o
            n = 4 * int(np.prod(shape[1:]))
            n = (n + 31) // 32 * 32
            t = at(name, shape, fp32, o)
            o += n / K
            return t

        gatesT = at("gates_T", [48, 256], fp32, 144)
        gates = small("gates", [128, TILES, 48])
        kcmp = small("k_cmp_T", [128, KV, 32])
        nmax = [small(f"neg_max{i}", [128, 4]) for i in range(2)]
        esum = [small(f"exp_sum{i}", [128, 4]) for i in range(2)]
        alpha = [small(f"alpha{i}", [128, 2, 4]) for i in range(2)]
        cst = small("cmp_stats", [128, 4, TILES * HEADS])
        assert o <= 160
        par = at("params", [128, PACK_W], fp32, 160)
        assert PACK_W * 4 <= 4 * K
        bcr = at("b_c_raw", [128, 4, PAIRS, 16], fp32, 164)
        BD = at("b_blocks", [128, 2, PAIRS, 32], fp32, 172)
        bias = at("bias_neg", [128, HEADS, 256], fp32, 164)
        biasc = at("bias_cmp_neg", [128, TILES, HEADS, CMP_PAD], fp32, 180)
        M = at("rot_prod", [128, 2, 2, 256], fp32, 182)
        W = at("rot_in", [128, 2, 256], fp32, 186)
        Z = [at(f"scan{i}", [128, 2, 256], fp32, 188 + 2 * i) for i in range(2)]
        N = [at(f"back_prod{i}", [128, 2, 2, 256], fp32, 192 + 4 * i) for i in range(2)]
        S = [at(f"state{i}", [128, 2, 256], fp32, 200 + 2 * i) for i in range(2)]
        ZH = at("z_hi", [128, OCTETS, 256], f32r, 182)
        ZL = at("z_lo", [128, OCTETS, 256], f32r, 190)
        oh = at("buckets", [BUCKETS + 1, DIST_W + BIAS_W + HEADS], fp32, 192)
        brow = at("bias_row", [HEADS, BIAS_W], fp32, 198)
        lcmp = biasc[:, :, :, :].rearrange("p t h n -> p (t h) n")
        coef = at("coefs", [128, 12, PAIRS], fp32, 182)
        bprod = at("b_prod", [128, 4, PAIRS, 16], fp32, 184)
        st = at("ssm_stay", [128, 2, PAIRS], fp32, 206)
        spare = at("spare", [128, 3], fp32, 206.375)
        rs = at("row_stats", [128, 4, 2], fp32, 206.5)
        parts = at("row_parts", [128, TILES, 4], fp32, 206.75)
        MH = at("mlp_hi", [128, 32, 256], f32r, 96)
        ML = at("mlp_lo", [128, 32, 256], f32r, 128)
        RT = [at(f"relu{i}", [128, 4, 256], fp32, 164 + 4 * i) for i in range(2)]
        SQ = [at(f"squared{i}", [128, 4, 256], fp32, 172 + 4 * i) for i in range(2)]
        NF = at("norm_f", [128, D], fp32, 182)
        junk_mlp = at("junk_mlp", [128, 512], fp32, 164)

        def P(name):
            return par[:, PACK[name][0]:PACK[name][1]]

        ident = P("ident")
        tv = P("tv")

        G = [ctx.enter_context(nc.psum_tensor(f"gemm{i}", [128, 2, 512], fp32)) for i in range(2)]
        BU = [ctx.enter_context(nc.psum_tensor(f"bu{i}", [128, 2, 256], fp32)) for i in range(2)]
        OB = ctx.enter_context(nc.psum_tensor("o_bank", [128, 512], fp32))
        YB = ctx.enter_context(nc.psum_tensor("y_bank", [128, 512], fp32))
        hid_ps = OB[0:64, :]
        TB = [BU[0][:, :, :].rearrange("p a b -> p (a b)"), BU[1][:, :, :].rearrange("p a b -> p (a b)"),
              OB[:, :], YB[:, :]]
        kc_ps = OB[:, 0:128]
        vc_ps = OB[:, 128:384].rearrange("p (v d) -> p v d", v=KV)
        YT = [OB[:, 0:256], YB[:, 0:256]]

        piece_in = [sem(f"piece_in{i}") for i in range(SLOTS)]
        x_in = [sem(f"x_in{i}") for i in range(4)]
        par_in, bc_in, oh_in, nf_in = (sem(n) for n in ("par_in", "bc_in", "oh_in", "nf_in"))
        hi_ready, lo_ready, piece_used = sem("hi_ready"), sem("lo_ready"), sem("piece_used")
        bias_row_ready, bias_out, bias_in, biasc_ready = (sem(n) for n in (
            "bias_row_ready", "bias_out", "bias_in", "biasc_ready"))
        bias_mm, zeroed, coef_step, coef_act = (sem(n) for n in ("bias_mm", "zeroed", "coef_step", "coef_act"))
        b_prod, b_blocks, b_T, b_T_out, c_blocks = (sem(n) for n in (
            "b_prod_done", "b_blocks_done", "b_T_done", "b_T_out", "c_blocks_done"))
        ss_ready, std_ready, rinv_ready, diag_ready = (sem(n) for n in (
            "ss_ready", "std_ready", "rinv_ready", "diag_ready"))
        own_sums = sem("own_sums")
        sum_ready, root_loaded, gate_T, rinv_squared = (sem(n) for n in (
            "sum_ready", "root_loaded", "gate_T", "rinv_squared"))
        h_tr, h_hi, h_lo = sem("h_tr"), sem("h_hi"), sem("h_lo")
        u_ready, kc_ready, q_ready, gate_ready, kv_ready = (sem(n) for n in (
            "u_ready", "kc_ready", "q_ready", "gate_ready", "kv_ready"))
        tab_work, tab_trig = sem("tab_work"), sem("tab_trig")
        bu_done, ssm_prod, ssm_rot, ssm_scan, ssm_back, ssm_state, y_done, y_out = (sem(n) for n in (
            "bu_done", "ssm_prod", "ssm_rot", "ssm_scan", "ssm_back", "ssm_state", "y_done", "y_out"))
        hidv_zero, cmp_zeroed = sem("hidv_zero"), sem("cmp_zeroed")
        flat_ready, hrow_ready, hid_T, pads = (sem(n) for n in ("flat_ready", "hrow_ready", "hid_T", "pads_zeroed"))
        hid_ready, cmp_kv, cmp_kv_out = (sem(n) for n in ("hid_ready", "cmp_kv", "cmp_kv_out"))
        cmp_logits, cmp_step, cmp_exp, cmp_T, cmp_T_out = (sem(n) for n in (
            "cmp_logits", "cmp_step", "cmp_exp", "cmp_T", "cmp_T_out"))
        qk_done, lg_ready, exp_ready, pT_done, pT_out, pv_done = (sem(n) for n in (
            "qk_done", "lg_ready", "exp_ready", "pT_done", "pT_out", "pv_done"))
        al_step, diag_out = sem("al_step"), sem("gate_diag_out")
        yt_hi, yt_lo = sem("yt_hi"), sem("yt_lo")
        z_ready, z_hi, z_lo = sem("z_ready"), sem("z_hi_done"), sem("z_lo_done")
        sg_ready, mix_ready, mix_hi, mix_lo = (sem(n) for n in ("sg_ready", "mix_ready", "mix_hi", "mix_lo"))
        x_added = sem("x_added")
        relu_ready, sq_ready, mlp_hi, mlp_lo = (sem(n) for n in ("relu_ready", "sq_ready", "mlp_hi_done", "mlp_lo_done"))
        gained = sem("gained")
        normed_0, normed_1, stored = (sem(n) for n in ("normed_0", "normed_1", "stored"))
        LEFT, LAST = (slice(0, 768), slice(768, 1536)), slice(1536, D)

        STEPS = []

        def pair_slot(k):
            if k % 2 == 0 and k // 2 + 1 < PAIRS // 2:
                STEPS.append(("tab", k // 2 + 1))
            if k % 2 == 1 and k // 2 + 1 < PAIRS // 2:
                STEPS.append(("trig", k // 2 + 1))
            if k + 1 < PAIRS:
                STEPS.append(("bu", k + 1))
            if k < PAIRS:
                STEPS.append(("rot", k))
                STEPS.append(("back", k))
            if 1 <= k <= PAIRS:
                STEPS.append(("state", k - 1))
            if k >= 3 and (k - 3) % 4 == 3:
                STEPS.append(("y_out", (k - 3) // 4))
            if k >= 2 and k - 2 < PAIRS:
                STEPS.append(("y", k - 2))
            if k == PAIRS + 1:
                STEPS.append(("y_out", OCTETS - 1))

        slots = iter(range(PAIRS + 2))
        PROD = [("in", c) for c in range(5)] + [("gate", 0), ("in", 5), ("in", 6)]
        prod_no = {p: i for i, p in enumerate(PROD)}
        AFTER = {("in", 0, 0): [("coef_trig", 0), ("coef", 0)], ("in", 0, 1): [("bias_c", 0), ("c_blocks", 0)],
                 ("in", 0, 2): [("b_blocks", 0)], ("in", 0, 3): [("tab", 0), ("b_T", 0)]}
        SLOT_END = {("in", 3, 1): [("flat", 0)], ("in", 3, 2): [("flat", 1)],
                    ("in", 4, 0): [("hidden", 0), ("hid_T", 0)],
                    ("in", 4, 1): [("hid_T_out", 0), ("cmp_kv", 0)], ("in", 4, 2): [("cmp_kv_out", 0)],
                    ("gate", 0, 0): [("cmp_l", 0)], ("in", 5, 0): [("cmp_l_out", 0), ("gate_T", 0)],
                    ("in", 5, 1): [("gate_out", 0), ("cmp_min", 0)],
                    ("in", 5, 2): [("cmp_exp", 0), ("cmp_p", 0)],
                    ("in", 6, 0): [("cmp_T", 0)],
                    ("in", 6, 1): [("cmp_T_out", 0)],
                    ("in", 6, 3): [("gelu", 0), ("gelu", 1)]}
        DOUBLE = (16, 18, 21, 24)
        pending = None
        for s, (kind, c, g) in enumerate(STREAM):
            if kind == "glu":
                break
            if s >= 2:
                STEPS.append(("split", s))
            STEPS.append(("product", s))
            if kind != "cmp" and pending is not None:
                STEPS.append(("evac", pending))
                if pending == 0:
                    STEPS.extend([("b_T_out", 0), ("trig", 0), ("bu", 0)])
                pending = None
            STEPS.extend(AFTER.get((kind, c, g), []))
            if kind == "gate" or (kind == "in" and g == 3):
                pending = prod_no[(kind, c)]
            for _ in range(0 if s < 5 else 2 if s in DOUBLE else 1):
                k = next(slots, None)
                if k is not None:
                    pair_slot(k)
            STEPS.extend(SLOT_END.get((kind, c, g), []))
        STEPS.append(("evac", pending))
        for k in slots:
            pair_slot(k)
        G0, O0 = first_piece[("glu", 0)], first_piece[("out", 0)]
        def split(s):
            STEPS.append(("split", s))

        AT_HEAD = dict(zip((2, 3, 4, 5, 9, 11, 13, 16, 17), range(G0, O0 + 5)))
        STEPS.append(("hi", G0))
        STEPS.extend([("gelu", 2), ("gelu", 3)])
        STEPS.append(("qk", 0))
        STEPS.append(("alpha", 0))
        STEPS.append(("lo", G0))
        STEPS.append(("z", 0))
        for h in range(1, HEADS + 2):
            if h < HEADS:
                STEPS.append(("qk", h))
            if h in AT_HEAD:
                split(AT_HEAD[h] + 1)
            if h > HEADS:
                STEPS.append(("product", AT_HEAD[h]))
            if h >= 2:
                STEPS.append(("pv", h - 2))
            if h >= 3 and h % 2 == 1:
                STEPS.append(("yT", (h - 3) // 2))
            if h in AT_HEAD and h <= HEADS:
                STEPS.append(("product", AT_HEAD[h]))
            if h <= HEADS:
                STEPS.append(("pT", h - 1))
            if h < HEADS:
                STEPS.append(("alpha", h))
            for c, last in enumerate((3, 5)):
                if last <= h < last + 4:
                    STEPS.append((("glu_gate", "glu_mul", "glu_hi", "glu_lo")[h - last], c))
        X_T_OUT = [8, 9, 15]
        for s in range(O0 + 5, O0 + 16):
            if s > O0 + 5:
                split(s)
            if s - O0 in X_T_OUT:
                STEPS.append(("x_T_out", X_T_OUT.index(s - O0)))
            STEPS.append(("product", s))
            for c in range(3):
                late = 1 if c == 0 else 0
                if s - O0 == out_end[c] + 1 + late:
                    STEPS.append(("add", c))
                    STEPS.append(("x_T", c))
                if s - O0 == out_end[c] + 2 + late:
                    STEPS.append(("sum", c))
        STEPS.extend([("mlp_split", 0), ("add", 3), ("mlp_split", 1), ("x_T_out", 3), ("mlp_split", 2), ("root", 0), ("sum", 3)])

        EVAC = {0: (u_ready, 2), 1: (u_ready, 4), 2: (kc_ready, 4), 3: (q_ready, 2), 4: (q_ready, 4),
                5: (gate_ready, 1), 6: (kv_ready, 5), 7: (kv_ready, 10)}

        block = ctx.enter_context(nc.Block())

        def compress_layout(copy, b, half):
            v = b[64 * half:64 * half + 64, :, :].rearrange("p a (m t q) -> p (a m) t q", m=2, q=2)
            for par_ in range(2):
                copy(kcat[64 * par_:64 * par_ + 64, 0:1024].rearrange("p (k h t) -> p k h t", h=2, t=128)[:, :, half, :],
                     v[:, :, :, par_], kc_ready)

        def key_layout(copy, b, a, half):
            for to in range(2):
                copy(kdup[a][64 * to:64 * to + 64, half::2, :],
                     b[64 * half:64 * half + 64, 0, :].rearrange("p (m t) -> p m t", m=2), kv_ready)

        @block.sync
        def _(sp):
            for j in range(2):
                for t in range(TILES):
                    sp.dma_start(X[:, t, j * 1024:(j + 1) * 1024],
                                 x_v[:, t, j * 1024:(j + 1) * 1024]).then_inc(x_in[2 * j + t], 16)

            def source(kind, c, g):
                if kind == "in":
                    n = IN_CHUNKS[c]
                    return w_in[g * 512:(g + 1) * 512, n * 512:(n + 1) * 512].rearrange("(k p) n -> p k n", p=128)
                if kind == "gate":
                    return w_in[:, 3584:D_IN].rearrange("(k p) n -> p k n", p=128)
                if kind == "cmp":
                    w = (w_ck1, w_cv1)[c]
                    return w[g * 1024:(g + 1) * 1024, :].rearrange("(k p) n -> p k n", p=128)
                w = w_glu if kind == "glu" else w_out
                return w[g * 512:(g + 1) * 512, c * 512:(c + 1) * 512].rearrange("(k p) n -> p k n", p=128)

            def load_piece(s):
                kind, c, g = STREAM[s]
                src = source(kind, c, g)
                if s >= SLOTS:
                    sp.wait_ge(piece_used, s - SLOTS + 1)
                n = src.shape[1] * src.shape[2]
                dst = raw[s % SLOTS][:, 0:n].rearrange("p (k n) -> p k n", n=src.shape[2])
                sp.dma_start(dst, src).then_inc(piece_in[s % SLOTS], 16)

            for s in range(N0):
                if s == O0 + 7:
                    sp.wait_ge(pv_done, HEADS - 1)
                    for j in range(2):
                        sp.dma_start(X[:, 1, j * 1024:(j + 1) * 1024],
                                     x_v[:, 1, j * 1024:(j + 1) * 1024]).then_inc(x_in[2 * j + 1], 16)
                load_piece(s)
                if s == 1:
                    sp.dma_start(bcr[:, :, :, :].rearrange("p a b c -> p (a b c)"), bc).then_inc(bc_in, 16)
                if s == 7:
                    sp.wait_ge(bias_out, 16)
                    sp.wait_ge(b_T_out, 4)
                    sp.wait_ge(c_blocks, 4)
                    sp.dma_start(bias[:, :, :], bass.AP(bias_dram.tensor, 127, [[BIAS_W, 128], [BIAS_PITCH, HEADS], [1, 256]])
                                 ).then_inc(bias_in, 16)
            sp.wait_ge(piece_used, first_piece[("glu", 1)] + 2)
            sp.dma_start(NF[:, :], nf.partition_broadcast(128)).then_inc(nf_in, 16)
            for f in range(2):
                up0 = N0 + 64 * f
                with sp.Fori(0, 8) as c:
                    for g in range(4):
                        slot = (up0 + g) % SLOTS
                        sp.wait_ge(piece_used, c * 4 + (up0 + g - SLOTS + 1))
                        sp.dma_start(raw[slot][:, :].rearrange("p (k n) -> p k n", n=512),
                                     w_up[g * 512:(g + 1) * 512, bass.ds(c * 512 + f * FF_HALF, 512)]
                                     .rearrange("(k p) n -> p k n", p=128)).then_inc(piece_in[slot], 16)
                dn0 = up0 + 32
                with sp.Fori(0, 4) as c:
                    for g in range(8):
                        slot = (dn0 + g) % SLOTS
                        sp.wait_ge(piece_used, c * 8 + (dn0 + g - SLOTS + 1))
                        sp.dma_start(raw[slot][:, :].rearrange("p (k n) -> p k n", n=512),
                                     w_down[f * FF_HALF + g * 512:f * FF_HALF + (g + 1) * 512, bass.ds(c * 512, 512)]
                                     .rearrange("(k p) n -> p k n", p=128)).then_inc(piece_in[slot], 16)
            for done, n, rows, cols in ((normed_0, 1, slice(0, 1), LEFT[0]), (normed_1, 1, slice(0, TILES), LAST),
                                        (normed_0, 2, slice(0, 1), LEFT[1]), (normed_1, 2, slice(1, 2), LEFT[0]),
                                        (normed_1, 3, slice(1, 2), LEFT[1])):
                sp.wait_ge(done, n)
                sp.dma_start(out_v[:, rows, cols], X[:, rows, cols]).then_inc(stored, 16)
            sp.wait_ge(stored, 16 * 5)

        @block.gpsimd
        def _(pool):
            pool.memset(CL[:, :, :, :], 0.0).then_inc(zeroed, 1)
            pool.memset(BD[:, :, :, :], 0.0).then_inc(zeroed, 1)
            pool.memset(hidk[:, :, :, :], 0.0).then_inc(zeroed, 1)
            pool.memset(kcat[:, 1024:1032], 0.0).then_inc(pads, 1)
            pool.memset(hidv[:, :, :, :, :], 0.0).then_inc(hidv_zero, 1)
            pool.wait_ge(bc_in, 16)
            pool.wait_ge(coef_step, COEF_N)
            for i, (cc, bb) in enumerate(((10, 0), (11, 1), (10, 1), (11, 0))):
                pool.tensor_tensor(bprod[:, i, :, :], bcr[:, bb, :, :],
                                   coef[:, cc, :].unsqueeze(2).to_broadcast([128, PAIRS, 16]),
                                   ALU.mult).then_inc(b_prod, 1)

            def table_turns(h):
                n = 5 * h
                if h >= 1:
                    pool.wait_ge(tab_trig, 3 * h)
                for j in range(2):
                    f = st[:, 1, 2 * h + j:2 * h + j + 1]
                    pool.tensor_scalar(turn[:, j, :], tv, f, 0.0, ALU.mult, ALU.add).then_inc(tab_work, 1)
                pool.wait_ge(tab_work, n + 2)
                pool.tensor_scalar(whole[:, :, :], turn[:, :, :], 1.0, MAGIC, ALU.mult, ALU.add).then_inc(tab_work, 1)
                pool.wait_ge(tab_work, n + 3)
                pool.tensor_scalar(whole[:, :, :], whole[:, :, :], -MAGIC, 1.0, ALU.add, ALU.mult).then_inc(tab_work, 1)
                pool.wait_ge(tab_work, n + 4)
                pool.tensor_tensor(turn[:, :, :], turn[:, :, :], whole[:, :, :], ALU.subtract).then_inc(tab_work, 1)

            def back_products(k):
                pool.wait_ge(ssm_scan, 2 * k + 2)
                if k == 0:
                    pool.wait_ge(bias_out, 16)
                    pool.wait_ge(bias_mm, 2)
                if k >= 2:
                    pool.wait_ge(ssm_state, 2 * (k - 1))
                cs = CS[(k // 2) % 2]
                for i in range(2):
                    pool.tensor_tensor(N[k % 2][:, i, :, :], Z[k % 2][:, :, :],
                                       cs[:, i, k % 2, :].unsqueeze(1).to_broadcast([128, 2, 256]),
                                       ALU.mult).then_inc(ssm_back, 1)

            for step, i in STEPS:
                if step == "tab":
                    table_turns(i)
                elif step == "back":
                    back_products(i)
                elif step == "c_blocks":
                    pool.wait_ge(h_tr, KT // 2)
                    pool.memset(vblk[:, :, :], 0.0).then_inc(cmp_zeroed, 1)
                    pool.memset(pcmp[:, :, :], 0.0).then_inc(cmp_zeroed, 1)
                elif step == "z":
                    for j in range(2, 4):
                        pool.wait_ge(z_hi, j + 1)
                        pool.tensor_tensor(ZL[:, 2 * j:2 * j + 2, :], uT[:, 2 * j:2 * j + 2, :],
                                           ZH[:, 2 * j:2 * j + 2, :].bitcast(fp32), ALU.subtract).then_inc(z_lo, 1)
                elif step == "alpha":
                    pool.wait_ge(al_step, 2 * i + 2)
                    if i >= 2:
                        pool.wait_ge(pT_done, 2 * (i - 1))
                    pool.tensor_tensor(dg[i % 2][:, :, :], ident.unsqueeze(1).to_broadcast([128, 4, 128]),
                                       alpha[i % 2][:, 1, :].unsqueeze(2).to_broadcast([128, 4, 128]),
                                       ALU.mult).then_inc(diag_out, 1)

        @block.scalar
        def _(act):
            act.dma_start(par[:, :], params).then_inc(par_in, 16)
            act.dma_start(oh[:, :], buckets).then_inc(oh_in, 16)

            eps_ap = rs[:, 2, 0:1]
            half_pi_ap = rs[:, 2, 1:2]

            def square_sum(junk_, v, part):
                nc.scalar.activation(junk_, v, ACT.Square, accum_out=part).then_inc(ss_ready, 1)

            def load_root(n):
                nc.scalar.activation(spare[:, n:n + 1], eps_ap, ACT.Sqrt).then_inc(root_loaded, 1)

            def root(n):
                act.wait_ge(sum_ready, n + 1)
                nc.scalar.activation(rs[:, 1, :], rs[:, 0, :], ACT.Sqrt, scale=1.0 / D,
                                     bias=eps_ap).then_inc(std_ready, 1)

            def h_transposed(n, gain, pairs=range(KT // 2)):
                for kp in pairs:
                    act.wait_ge(h_tr, 8 * n + kp + 1)
                    for j in range(2):
                        k = 2 * kp + j
                        nc.scalar.activation(AH[:, k, :], TB[kp % 4][:, j * 256:(j + 1) * 256], ACT.Copy,
                                             scale=gain[:, k:k + 1]).then_inc(h_hi, 1)

            def split_hi(s, no, slot_value):
                slot = s % SLOTS
                act.wait_ge(piece_in[slot], slot_value)
                if no >= 2:
                    act.wait_ge(piece_used, used_before(no - 2))
                n = width(s)
                nc.scalar.activation(whi[no % 2][:, 0:n], raw[slot][:, 0:n], ACT.Copy).then_inc(hi_ready, 1)

            split_piece = [s for s in range(N0) if is_split[s]]

            def first_splits():
                split_hi(0, 0, 16)
                h_transposed(0, P("n1"), range(0, KT // 4))
                split_hi(1, 1, 16)
                h_transposed(0, P("n1"), range(KT // 4, KT // 2))

            def used_before(no):
                return split_piece[no] + 1

            act.wait_ge(par_in, 16)
            nc.scalar.activation(coef[:, 0, :], P("ldt"), ACT.Exp).then_inc(coef_act, 1)
            act.wait_ge(coef_step, 2)
            nc.scalar.activation(st[:, 0, :], coef[:, 1, :], ACT.Exp).then_inc(coef_act, 1)
            load_root(0)
            act.wait_ge(bias_mm, 1)
            nc.scalar.activation(brow[:, :], G[0][0:HEADS, 0, 0:BIAS_W], ACT.Copy, scale=-1.0).then_inc(bias_row_ready, 1)
            act.wait_ge(bias_row_ready, 1)
            act.dma_start(bass.AP(bias_dram.tensor, 0, [[BIAS_PITCH, HEADS], [BIAS_W + 1, 128], [1, BIAS_W]]),
                          brow[:, :].unsqueeze(1).to_broadcast([HEADS, 128, BIAS_W])).then_inc(bias_out, 16)
            for j in range(2):
                act.wait_ge(x_in[2 * j], 16)
                if j:
                    act.wait_ge(ss_ready, 1)
                square_sum(junk[0][:, :], X[:, 0, 1024 * j:1024 * j + 1024], parts[:, 0, j:j + 1])
            root(0)
            first_splits()

            def evac(g):
                b = G[g % 2]
                kind, c = PROD[g]
                s_last = first_piece[(kind, c)] + (0 if kind == "gate" else 3)
                act.wait_ge(piece_used, s_last + 1)
                if kind == "gate":
                    nc.scalar.activation(gatesT[:, :], b[0:48, 0, 0:256], ACT.Sigmoid).then_inc(gate_T, 1)
                elif c < 2:
                    for j in range(2):
                        nc.scalar.activation(uT[:, 4 * c + 2 * j:4 * c + 2 * j + 2, :],
                                             b[:, j, :].rearrange("p (m t) -> p m t", m=2), ACT.Copy
                                             ).then_inc(u_ready, 1)
                elif c in (3, 4):
                    for j in range(2):
                        m = 4 * (c - 3) + 2 * j
                        nc.scalar.activation(qT[:, m:m + 2, :], b[:, j, :].rearrange("p (m t) -> p m t", m=2),
                                             ACT.Copy, scale=-(HD ** -0.5)).then_inc(q_ready, 1)
                elif c == 2:
                    compress_layout(act_copy, b, 0)
                else:
                    key_layout(act_copy, b, c - 5, 0)
                    nc.scalar.activation(vrow[c - 5][:, :, :], b[:, 1, :].rearrange("p (t n) -> p t n", t=2),
                                         ACT.Copy).then_inc(kv_ready, 1)

            def act_copy(dst, src, signal):
                nc.scalar.activation(dst, src, ACT.Copy).then_inc(signal, 1)

            def table_trig(h):
                act.wait_ge(tab_work, 5 * h + 5)
                if h >= 2:
                    act.wait_ge(ssm_back, 4 * (h - 1))
                cs = CS[h % 2]
                nc.scalar.activation(cs[:, 1, :, :], turn[:, :, :], ACT.Sin, scale=TWO_PI_DOWN).then_inc(tab_trig, 1)
                nc.scalar.activation(whole[:, :, :], turn[:, :, :], ACT.Abs).then_inc(tab_trig, 1)
                act.wait_ge(tab_trig, 3 * h + 2)
                nc.scalar.activation(cs[:, 0, :, :], whole[:, :, :], ACT.Sin, scale=-TWO_PI_DOWN,
                                     bias=half_pi_ap).then_inc(tab_trig, 1)

            def mlp_split(i, base, j, per):
                s = base + j
                no = SP0 + (base - N0) + j
                slot = s % SLOTS
                act.wait_ge(piece_in[slot], i * (4 * per) + 16 * (s // SLOTS + 1))
                act.wait_ge(piece_used, i * per + (s - 1))
                nc.scalar.activation(whi[no % 2][:, :], raw[slot][:, :], ACT.Copy).then_inc(hi_ready, 1)

            for step, i in STEPS:
                if step in ("split", "hi"):
                    if is_split[i]:
                        split_hi(i, split_no[i], 16 * (i // SLOTS + 1))
                elif step == "evac":
                    evac(i)
                elif step == "trig":
                    table_trig(i)
                elif step == "bias_c":
                    act.wait_ge(bias_mm, 2)
                    v = G[1][:, 1, 0:CMP_PAD * HEADS].rearrange("p (n h) -> p h n", h=HEADS)
                    half = CMP_PAD // 2
                    for dst, src in ((biasc[:, 1, :, :], v), (biasc[:, 0, :, 0:half], v[:, :, half:]),
                                     (biasc[:, 0, :, half:], v[:, :, CMP_PAD - 1:].to_broadcast([128, HEADS, half]))):
                        nc.scalar.activation(dst, src, ACT.Copy, scale=-1.0).then_inc(biasc_ready, 1)
                elif step == "coef_trig":
                    nc.scalar.activation(coef[:, 4, :], st[:, 1, :], ACT.Sin, scale=TWO_PI_DOWN).then_inc(coef_act, 1)
                    nc.scalar.activation(coef[:, 2, :], st[:, 1, :], ACT.Abs).then_inc(coef_act, 1)
                    act.wait_ge(coef_act, 4)
                    nc.scalar.activation(coef[:, 5, :], coef[:, 2, :], ACT.Sin, scale=-TWO_PI_DOWN,
                                         bias=half_pi_ap).then_inc(coef_act, 1)
                elif step == "b_T_out":
                    for r in range(2):
                        for j in range(2):
                            act.wait_ge(b_T, 2 * r + j + 1)
                            nc.scalar.activation(BL[:, 4 * j:4 * j + 4, r, :],
                                                 TB[2 * r + j].rearrange("p (b n) -> p b n", b=4),
                                                 ACT.Copy).then_inc(b_T_out, 1)
                elif step == "hidden":
                    act.wait_ge(piece_used, first_piece[("cmp", 1)] + 2)
                    nc.scalar.activation(hrow[:, :], hid_ps, ACT.Gelu_apprx_tanh).then_inc(hrow_ready, 1)
                elif step == "hid_T_out":
                    act.wait_ge(hid_T, 1)
                    act.wait_ge(zeroed, 3)
                    act.wait_ge(hidv_zero, 1)
                    src = OB[:, 0:128].rearrange("p (j v n) -> p j v n", j=2, v=KV)
                    nc.scalar.activation(hidk[:, :, :, 0:CMP_PAD].rearrange("p j v n -> p (j v) n"),
                                         src.rearrange("p j v n -> p (j v) n"), ACT.Copy).then_inc(hid_ready, 1)
                    for j in range(2):
                        src = OB[:, 128 + 64 * j:192 + 64 * j].rearrange("p (v n) -> p v n", v=KV)
                        nc.scalar.activation(hidv[:, j, :, :, 0:CMP_PAD],
                                             src.unsqueeze(2).to_broadcast([128, KV, 4, CMP_PAD]),
                                             ACT.Copy).then_inc(hid_ready, 1)
                elif step == "cmp_kv_out":
                    act.wait_ge(cmp_kv, 2)
                    src = kc_ps.rearrange("p (v n) -> p v n", v=KV)
                    for dst, v in ((kcmp[0:64, :, :], src[0:64, :, :]), (kcmp[64:128, :, 16:32], src[64:128, :, 0:16]),
                                   (kcmp[64:128, :, 0:16], src[64:128, :, 16:32])):
                        nc.scalar.activation(dst, v, ACT.Copy).then_inc(cmp_kv_out, 1)
                elif step == "gate_out":
                    act.wait_ge(gate_T, 2)
                    nc.scalar.activation(gates[:, :, :], G[1][:, 1, 0:96].rearrange("p (t n) -> p t n", t=2),
                                         ACT.Copy).then_inc(gate_ready, 1)
                elif step == "cmp_exp":
                    act.wait_ge(cmp_step, 3)
                    nc.scalar.activation(lcmp, lcmp, ACT.Exp, scale=-1.0).then_inc(cmp_exp, 1)
                elif step == "cmp_T_out":
                    act.wait_ge(cmp_T, 1)
                    for t in range(TILES):
                        nc.scalar.activation(pcT[:, :, t, :], G[0][:, t, :].rearrange("p (k q) -> p k q", q=128),
                                             ACT.Copy).then_inc(cmp_T_out, 1)
                elif step == "gelu":
                    act.wait_ge(y_out, 2 * i + 2)
                    v = uT[:, 2 * i:2 * i + 2, :]
                    nc.scalar.activation(v, v, ACT.Gelu_apprx_tanh).then_inc(z_ready, 1)
                elif step == "z":
                    for j in range(4):
                        act.wait_ge(z_ready, 4)
                        nc.scalar.activation(ZH[:, 2 * j:2 * j + 2, :], uT[:, 2 * j:2 * j + 2, :], ACT.Copy).then_inc(z_hi, 1)
                elif step == "glu_gate":
                    c = i
                    act.wait_ge(piece_used, G0 + 2 * c + 2)
                    for m in range(4):
                        n = 4 * c + m
                        nc.scalar.activation(mixv[c][:, m, :], G[1][:, m // 2, (m % 2) * 256:(m % 2 + 1) * 256],
                                             ACT.Sigmoid, bias=P("bglu")[:, n:n + 1]).then_inc(sg_ready, 1)
                elif step == "glu_hi":
                    c = i
                    act.wait_ge(mix_ready, c + 1)
                    nc.scalar.activation(AH[:, 4 * c:4 * c + 4, :], mixv[c][:, :, :], ACT.Copy).then_inc(mix_hi, 1)
                elif step == "yT":
                    act.wait_ge(pv_done, 2 * i + 2)
                    nc.scalar.activation(AH[:, 8 + i, :], YT[i % 2], ACT.Copy).then_inc(yt_hi, 1)
                elif step == "mlp_split":
                    mlp_split(0, N0, i, 0)
                elif step == "x_T_out":
                    for kp in range(2 * i, 2 * i + 2):
                        act.wait_ge(h_tr, 8 + kp + 1)
                        if i == 2:
                            act.wait_ge(piece_used, O0 + 14)
                        for j in range(2):
                            k = 2 * kp + j
                            nc.scalar.activation(h2(0, k), TB[kp % 4][:, j * 256:(j + 1) * 256], ACT.Copy,
                                                 scale=P("n2")[:, k:k + 1]).then_inc(h_hi, 1)
                elif step == "root":
                    load_root(1)
                elif step == "sum":
                    for t in range(TILES):
                        act.wait_ge(x_added, 2 * i + t + 1)
                        act.wait_ge(ss_ready, 2 + 2 * i + t)
                        square_sum(junk[0][:, 0:512], X[:, t, 512 * i:512 * i + 512], parts[:, t, i:i + 1])
                elif step == "qk":
                    h = i
                    for a in range(2):
                        for t in (1, 0):
                            j = 4 * h + 2 * a + (1 - t)
                            act.wait_ge(lg_ready, j + 1)
                            if h >= 2 and a == 0 and t == 1:
                                act.wait_ge(pT_done, 2 * (h - 1))
                                act.wait_ge(al_step, 2 * (h - 1))
                            cols = slice(0, 256) if t else slice(256, 384)
                            nc.scalar.activation(prob[h % 2][:, a, cols], lg[h % 2][:, a, cols], ACT.Exp, scale=-1.0,
                                                 bias=nmax[h % 2][:, 2 * a + t:2 * a + t + 1],
                                                 accum_out=esum[h % 2][:, 2 * a + t:2 * a + t + 1]
                                                 ).then_inc(exp_ready, 1)
                elif step == "pT":
                    act.wait_ge(pT_done, 2 * i + 1)
                    if i >= 2:
                        act.wait_ge(pv_done, i - 1)
                    nc.scalar.activation(pT[i % 2][:, 0, :], TB[0][:, 0:384], ACT.Copy).then_inc(pT_out, 1)

            def last_sums(c):
                for t in range(TILES):
                    act.wait_ge(x_added, 16 + 2 * c + t + 1)
                    act.wait_ge(ss_ready, 10 + 2 * c + t)
                    square_sum(junk_mlp[:, :], X[:, t, 512 * c:512 * c + 512], parts[:, t, c:c + 1])

            def relu(i, f, c, per):
                act.wait_ge(piece_used, i * (4 * per) + (N0 + 64 * f + 4 * c + 4))
                if f or c > 0:
                    act.wait_ge(sq_ready, i * per + max(8 * f + c - 1, 1))
                nc.scalar.activation(RT[c % 2][:, :, :].rearrange("p m t -> p (m t)"),
                                     G[(c + 1) % 2][:, :, :].rearrange("p a n -> p (a n)"),
                                     ACT.Relu).then_inc(relu_ready, 1)

            def squared_hi(i, f, c, per, dst):
                act.wait_ge(sq_ready, i * per + (8 * f + c + 1))
                if f and isinstance(i, int) and c == 0:
                    act.wait_ge(piece_used, N0 + 64)
                nc.scalar.activation(dst, SQ[c % 2][:, :, :], ACT.Copy).then_inc(mlp_hi, 1)

            for f in range(2):
                up0 = N0 + 64 * f
                for j in range(8):
                    if f or j >= 3:
                        mlp_split(0, up0, j, 0)
                    if f == 0 and j == 3:
                        root(1)
                    if j == 4:
                        relu(0, f, 0, 0)
                    if j == 5:
                        squared_hi(0, f, 0, 0, MH[:, 0:4, :])
                with act.Fori(0, 3) as i:
                    for j in range(8):
                        mlp_split(i, up0 + 8, j, 8)
                        if j == 0:
                            relu(i, f, 1, 2)
                        if j == 1:
                            squared_hi(i, f, 1, 2, MH[:, bass.ds(i * 8 + 4, 4), :])
                        if j == 4:
                            relu(i, f, 2, 2)
                        if j == 5:
                            squared_hi(i, f, 2, 2, MH[:, bass.ds(i * 8 + 8, 4), :])
                dn0 = up0 + 32
                mlp_split(0, dn0, 0, 0)
                relu(0, f, 7, 0)
                mlp_split(0, dn0, 1, 0)
                squared_hi(0, f, 7, 0, MH[:, 28:32, :])
                for j in range(2, 8):
                    mlp_split(0, dn0, j, 0)
                if f == 0:
                    with act.Fori(0, 3) as i:
                        for j in range(8):
                            mlp_split(i, dn0 + 8, j, 8)
                else:
                    for c in range(1, 4):
                        for j in range(8):
                            mlp_split(0, dn0 + 8 * c, j, 0)
                            if j == 1:
                                last_sums(c - 1)
            load_root(2)
            last_sums(3)
            root(2)
            act.wait_ge(rinv_ready, 3)
            act.wait_ge(gained, 6)
            for cols in LEFT:
                v = X[:, 0, cols]
                nc.scalar.activation(v, v, ACT.Copy, scale=rs[:, 1, 0:1]).then_inc(normed_0, 1)

        @block.vector
        def _(dve):
            V = nc.vector
            V.memset(rs[:, 2, 0:1], EPS).then_inc(coef_step, 1)
            V.memset(rs[:, 2, 1:2], math.pi / 2).then_inc(zeroed, 1)
            n = [1]

            def link(ins):
                n[0] += 1
                ins.then_inc(coef_step, 1)
                dve.wait_ge(coef_step, n[0])

            c = coef
            dve.wait_ge(par_in, 16)
            dve.wait_ge(coef_act, 1)
            link(V.tensor_tensor(c[:, 1, :], c[:, 0, :], P("are"), ALU.mult))
            link(V.tensor_tensor(c[:, 3, :], c[:, 0, :], P("aim"), ALU.mult))
            link(V.tensor_scalar(c[:, 6, :], c[:, 3, :], INV_2PI, MAGIC, ALU.mult, ALU.add))
            link(V.tensor_scalar(c[:, 6, :], c[:, 6, :], -MAGIC, None, ALU.add))
            link(V.scalar_tensor_tensor(out=c[:, 7, :], in0=c[:, 6, :], scalar=-C1, in1=c[:, 3, :],
                                        op0=ALU.mult, op1=ALU.add))
            link(V.scalar_tensor_tensor(out=c[:, 8, :], in0=c[:, 6, :], scalar=-C2, in1=c[:, 7, :],
                                        op0=ALU.mult, op1=ALU.add))
            link(V.scalar_tensor_tensor(out=c[:, 7, :], in0=c[:, 6, :], scalar=-C3, in1=c[:, 8, :],
                                        op0=ALU.mult, op1=ALU.add))
            link(V.tensor_scalar(c[:, 8, :], c[:, 7, :], INV_2PI, 0.5, ALU.mult, ALU.min))
            link(V.tensor_scalar(st[:, 1, :], c[:, 8, :], -0.5, None, ALU.max))

            def row_scales(k, n_parts):
                V.tensor_reduce(out=rs[:, 0, :], in_=parts[:, :, 0:n_parts], axis=AX.X, op=ALU.add).then_inc(sum_ready, 1)
                dve.wait_ge(std_ready, k + 1)
                V.reciprocal(rs[:, 1, :], rs[:, 1, :]).then_inc(rinv_ready, 1)
                dve.wait_ge(rinv_ready, k + 1)
                if k == 1:
                    V.tensor_tensor(rs[:, 3, :], rs[:, 1, :], rs[:, 1, :], ALU.mult).then_inc(rinv_squared, 1)
                if k == 0:
                    for t in range(TILES):
                        V.tensor_scalar(diag[:, t, :], ident, rs[:, 1, t:t + 1], None, ALU.mult).then_inc(diag_ready, 1)

            def h_transposed(k, gain, tiles=range(KT)):
                for kt in tiles:
                    kp = kt // 2
                    dve.wait_ge(h_hi, 16 * k + 2 * kp + 2)
                    V.scalar_tensor_tensor(out=AL[:, kt, :], in0=TB[kp % 4][:, (kt % 2) * 256:(kt % 2 + 1) * 256],
                                           scalar=gain[:, kt:kt + 1], in1=AH[:, kt, :].bitcast(fp32), op0=ALU.mult,
                                           op1=ALU.subtract).then_inc(h_lo, 1)

            for j in range(2):
                dve.wait_ge(x_in[2 * j + 1], 16)
                v = X[:, 1, 1024 * j:1024 * j + 1024]
                V.tensor_tensor_reduce(out=junk[1][:, :], in0=v, in1=v, scale=1.0, scalar=0.0,
                                       op0=ALU.mult, op1=ALU.add, accum_out=parts[:, 1, j:j + 1]).then_inc(own_sums, 1)
                dve.wait_ge(own_sums, j + 1)
            dve.wait_ge(ss_ready, 2)
            row_scales(0, 2)

            def coefficients():
                dve.wait_ge(coef_act, 5)
                link(V.tensor_tensor(c[:, 2, :], st[:, 0, :], c[:, 4, :], ALU.mult))
                link(V.tensor_tensor(c[:, 5, :], st[:, 0, :], c[:, 5, :], ALU.mult))
                link(V.tensor_scalar(c[:, 5, :], c[:, 5, :], -1.0, None, ALU.add))
                link(V.tensor_tensor(c[:, 6, :], P("are"), P("are"), ALU.mult))
                link(V.tensor_tensor(c[:, 7, :], P("aim"), P("aim"), ALU.mult))
                link(V.tensor_tensor(c[:, 6, :], c[:, 6, :], c[:, 7, :], ALU.add))
                link(V.reciprocal(c[:, 6, :], c[:, 6, :]))
                link(V.tensor_tensor(c[:, 7, :], c[:, 5, :], P("are"), ALU.mult))
                link(V.tensor_tensor(c[:, 8, :], c[:, 2, :], P("aim"), ALU.mult))
                link(V.tensor_tensor(c[:, 7, :], c[:, 7, :], c[:, 8, :], ALU.add))
                link(V.tensor_tensor(c[:, 10, :], c[:, 7, :], c[:, 6, :], ALU.mult))
                link(V.tensor_tensor(c[:, 7, :], c[:, 2, :], P("are"), ALU.mult))
                link(V.tensor_tensor(c[:, 8, :], c[:, 5, :], P("aim"), ALU.mult))
                link(V.tensor_tensor(c[:, 7, :], c[:, 7, :], c[:, 8, :], ALU.subtract))
                link(V.tensor_tensor(c[:, 11, :], c[:, 7, :], c[:, 6, :], ALU.mult))
                assert n[0] == COEF_N

            def c_in_blocks():
                dve.wait_ge(zeroed, 4)
                dve.wait_ge(bc_in, 16)
                for half in range(2):
                    p = slice(64 * half, 64 * half + 64)
                    w = slice(16 * half, 16 * half + 16)
                    V.tensor_copy(CL[p, 0, :, w], bcr[p, 2, :, :]).then_inc(c_blocks, 1)
                    V.tensor_scalar(CL[p, 1, :, w], bcr[p, 3, :, :], -1.0, None, ALU.mult).then_inc(c_blocks, 1)

            def b_in_blocks():
                dve.wait_ge(b_prod, 4)
                for half in range(2):
                    p = slice(64 * half, 64 * half + 64)
                    w = slice(16 * half, 16 * half + 16)
                    V.tensor_tensor(BD[p, 0, :, w], bprod[p, 0, :, :], bprod[p, 1, :, :], ALU.subtract).then_inc(b_blocks, 1)
                    V.tensor_tensor(BD[p, 1, :, w], bprod[p, 2, :, :], bprod[p, 3, :, :], ALU.add).then_inc(b_blocks, 1)

            def split_lo(s, no):
                dve.wait_ge(hi_ready, no + 1)
                n = width(s)
                V.tensor_tensor(wlo[s % SLOTS][:, 0:n], raw[s % SLOTS][:, 0:n], whi[no % 2][:, 0:n].bitcast(fp32),
                                ALU.subtract).then_inc(lo_ready, 1)

            split_lo(0, 0)
            h_transposed(0, P("n1"), range(0, KT // 2))
            split_lo(1, 1)
            h_transposed(0, P("n1"), range(KT // 2, KT))

            def rotate_and_scan(k):
                cs = CS[(k // 2) % 2]
                r = st[:, 0, k:k + 1].to_broadcast([128, 256])
                dve.wait_ge(bu_done, k + 1)
                dve.wait_ge(tab_trig, 3 * (k // 2 + 1))
                if k >= 1:
                    dve.wait_ge(ssm_rot, 2 * k)
                for i in range(2):
                    V.tensor_tensor(M[:, i, :, :], BU[k % 2][:, :, :],
                                    cs[:, i, k % 2, :].unsqueeze(1).to_broadcast([128, 2, 256]),
                                    ALU.mult).then_inc(ssm_prod, 1)
                dve.wait_ge(ssm_prod, 2 * k + 2)
                if k >= 1:
                    dve.wait_ge(ssm_scan, 2 * k)
                V.tensor_tensor(W[:, 0, :], M[:, 0, 0, :], M[:, 1, 1, :], ALU.add).then_inc(ssm_rot, 1)
                V.tensor_tensor(W[:, 1, :], M[:, 0, 1, :], M[:, 1, 0, :], ALU.subtract).then_inc(ssm_rot, 1)
                if k >= 2:
                    dve.wait_ge(ssm_back, 2 * (k - 1))
                for i in range(2):
                    dve.wait_ge(ssm_rot, 2 * k + i + 1)
                    V.tensor_tensor_scan(Z[k % 2][:, i, :], r, W[:, i, :], 0.0, ALU.mult, ALU.add).then_inc(ssm_scan, 1)

            def turned_states(k):
                dve.wait_ge(ssm_back, 2 * k + 2)
                if k >= 2:
                    dve.wait_ge(y_done, k - 1)
                b = N[k % 2]
                V.tensor_tensor(S[k % 2][:, 0, :], b[:, 0, 0, :], b[:, 1, 1, :], ALU.subtract).then_inc(ssm_state, 1)
                V.tensor_tensor(S[k % 2][:, 1, :], b[:, 0, 1, :], b[:, 1, 0, :], ALU.add).then_inc(ssm_state, 1)

            def octet_out(q):
                dve.wait_ge(y_done, 4 * q + 4)
                V.scalar_tensor_tensor(out=uT[:, q, :], in0=uT[:, q, :], scalar=P("d")[:, q:q + 1],
                                       in1=YB[:, (q % 2) * 256:(q % 2 + 1) * 256], op0=ALU.mult,
                                       op1=ALU.add).then_inc(y_out, 1)

            def dve_copy(dst, src, signal):
                V.tensor_copy(dst, src).then_inc(signal, 1)

            CM = [0]

            def cmp_link(ins):
                CM[0] += 1
                ins.then_inc(cmp_step, 1)
                dve.wait_ge(cmp_step, CM[0])

            def mlp_split(i, base, j, per):
                no = SP0 + (base - N0) + j
                dve.wait_ge(hi_ready, i * per + (no + 1))
                slot = (base + j) % SLOTS
                V.tensor_tensor(wlo[slot][:, :], raw[slot][:, :], whi[no % 2][:, :].bitcast(fp32),
                                ALU.subtract).then_inc(lo_ready, 1)

            TH = TILES * HEADS
            for step, i in STEPS:
                if step in ("split", "lo"):
                    if is_split[i]:
                        split_lo(i, split_no[i])
                elif step == "evac":
                    kind, cc = PROD[i]
                    if kind == "in" and cc in (2, 5, 6):
                        dve.wait_ge(piece_used, first_piece[(kind, cc)] + 4)
                        if cc == 2:
                            compress_layout(dve_copy, G[i % 2], 1)
                        else:
                            key_layout(dve_copy, G[i % 2], cc - 5, 1)
                elif step == "coef":
                    coefficients()
                elif step == "c_blocks":
                    c_in_blocks()
                elif step == "b_blocks":
                    b_in_blocks()
                elif step == "flat":
                    dve.wait_ge(kc_ready, 4)
                    dve.wait_ge(pads, 1)
                    v = kcat[:, 512 * i:512 * i + 16]
                    win = bass.AP(v.tensor, v.offset, [list(v.ap[0]), [1, KT], [8, 64]])
                    V.tensor_tensor(flat[:, i, :, :], win, P("pek" if i == 0 else "pev").unsqueeze(2)
                                    .to_broadcast([128, KT, 64]), ALU.add).then_inc(flat_ready, 1)
                elif step == "rot":
                    rotate_and_scan(i)
                elif step == "state":
                    turned_states(i)
                elif step == "y_out":
                    octet_out(i)
                elif step == "cmp_kv_out":
                    dve.wait_ge(cmp_zeroed, 2)
                    dve.wait_ge(cmp_kv_out, 3)
                    for r in range(4):
                        p = slice(32 * r, 32 * r + 32)
                        V.tensor_copy(vblk[p, :, HD * r:HD * r + HD], vc_ps[p, :, :]).then_inc(cmp_kv_out, 1)
                elif step == "cmp_l_out":
                    dve.wait_ge(cmp_logits, 1)
                    cmp_link(V.tensor_tensor(lcmp, OB[:, :].rearrange("p (k n) -> p k n", n=CMP_PAD), lcmp, ALU.add))
                elif step == "cmp_min":
                    cmp_link(V.tensor_reduce(out=cst[:, 0, :], in_=lcmp, axis=AX.X, op=ALU.min))
                    cmp_link(V.tensor_tensor(lcmp, lcmp, cst[:, 0, :].unsqueeze(2).to_broadcast([128, TH, CMP_PAD]),
                                             ALU.subtract))
                elif step == "cmp_p":
                    dve.wait_ge(cmp_exp, 1)
                    cmp_link(V.tensor_reduce(out=cst[:, 1, :], in_=lcmp, axis=AX.X, op=ALU.add))
                    cmp_link(V.reciprocal(cst[:, 2, :], cst[:, 1, :]))
                    dve.wait_ge(gate_ready, 1)
                    for t in range(TILES):
                        cmp_link(V.scalar_tensor_tensor(
                            out=cst[:, 3, t * HEADS:(t + 1) * HEADS], in0=cst[:, 2, t * HEADS:(t + 1) * HEADS],
                            scalar=P("valid")[:, t:t + 1],
                            in1=gates[:, t, :].rearrange("p (h i) -> p h i", i=3)[:, :, 0],
                            op0=ALU.mult, op1=ALU.mult))
                    cmp_link(V.tensor_tensor(pcmp[:, :, 0:CMP_PAD], lcmp,
                                             cst[:, 3, :].unsqueeze(2).to_broadcast([128, TH, CMP_PAD]), ALU.mult))
                elif step == "qk":
                    h = i
                    dve.wait_ge(qk_done, h + 1)
                    if h == 0:
                        dve.wait_ge(bias_in, 16)
                    if h >= 2:
                        dve.wait_ge(exp_ready, 4 * (h - 1))
                    for a in range(2):
                        for t in (1, 0):
                            cols = slice(0, 256) if t else slice(256, 384)
                            b = bias[:, h, :] if t else bias[:, h, 128:256]
                            V.tensor_tensor_reduce(out=lg[h % 2][:, a, cols], in0=G[0][:, a, cols], in1=b, scale=1.0,
                                                   scalar=3.0e38, op0=ALU.add, op1=ALU.min,
                                                   accum_out=nmax[h % 2][:, 2 * a + t:2 * a + t + 1]
                                                   ).then_inc(lg_ready, 1)
                elif step == "pT":
                    dve.wait_ge(pT_done, 2 * i + 2)
                    if i >= 2:
                        dve.wait_ge(pv_done, i - 1)
                    V.tensor_copy(pT[i % 2][:, 1, :], TB[1][:, 0:384]).then_inc(pT_out, 1)
                elif step == "alpha":
                    h = i
                    dve.wait_ge(exp_ready, 4 * h + 4)
                    if h >= 2:
                        dve.wait_ge(diag_out, h - 1)
                    V.reciprocal(alpha[h % 2][:, 0, :], esum[h % 2][:, :]).then_inc(al_step, 1)
                    dve.wait_ge(al_step, 2 * h + 1)
                    gv = gates[:, :, 3 * h + 1:3 * h + 3].rearrange("p t a -> p a t")
                    V.tensor_tensor(alpha[h % 2][:, 1, :].rearrange("p (a t) -> p a t", a=2),
                                    alpha[h % 2][:, 0, :].rearrange("p (a t) -> p a t", a=2), gv,
                                    ALU.mult).then_inc(al_step, 1)
                elif step == "z":
                    for j in range(2):
                        dve.wait_ge(z_hi, j + 1)
                        V.tensor_tensor(ZL[:, 2 * j:2 * j + 2, :], uT[:, 2 * j:2 * j + 2, :],
                                        ZH[:, 2 * j:2 * j + 2, :].bitcast(fp32), ALU.subtract).then_inc(z_lo, 1)
                elif step == "glu_mul":
                    dve.wait_ge(sg_ready, 4 * i + 4)
                    V.tensor_tensor(mixv[i][:, :, :], mixv[i][:, :, :], uT[:, 4 * i:4 * i + 4, :],
                                    ALU.mult).then_inc(mix_ready, 1)
                elif step == "glu_lo":
                    dve.wait_ge(mix_hi, i + 1)
                    V.tensor_tensor(AL[:, 4 * i:4 * i + 4, :], mixv[i][:, :, :],
                                    AH[:, 4 * i:4 * i + 4, :].bitcast(fp32), ALU.subtract).then_inc(mix_lo, 1)
                elif step == "yT":
                    dve.wait_ge(yt_hi, i + 1)
                    V.tensor_tensor(AL[:, 8 + i, :], YT[i % 2], AH[:, 8 + i, :].bitcast(fp32),
                                    ALU.subtract).then_inc(yt_lo, 1)
                elif step == "mlp_split":
                    mlp_split(0, N0, i, 0)
                elif step == "x_T_out":
                    for k in range(4 * i, 4 * i + 4):
                        kp = k // 2
                        dve.wait_ge(h_hi, 16 + 2 * kp + 2)
                        V.scalar_tensor_tensor(out=h2(1, k), in0=TB[kp % 4][:, (k % 2) * 256:(k % 2 + 1) * 256],
                                               scalar=P("n2")[:, k:k + 1], in1=h2(0, k).bitcast(fp32), op0=ALU.mult,
                                               op1=ALU.subtract).then_inc(h_lo, 1)
                elif step == "add":
                    dve.wait_ge(piece_used, O0 + out_end[i] + 1)
                    if i == 0:
                        for j in range(2):
                            dve.wait_ge(x_in[2 * j + 1], 32)
                    for t in range(TILES):
                        v = X[:, t, 512 * i:512 * i + 512]
                        V.tensor_tensor(v, v, G[(i + 1) % 2][:, t, :], ALU.add).then_inc(x_added, 1)

            def square(i, f, cc, per):
                dve.wait_ge(relu_ready, i * per + (8 * f + cc + 1))
                if f or cc > 0:
                    dve.wait_ge(mlp_lo, i * per + max(8 * f + cc - 1, 1))
                V.tensor_tensor(SQ[cc % 2][:, :, :], RT[cc % 2][:, :, :], RT[cc % 2][:, :, :],
                                ALU.mult).then_inc(sq_ready, 1)

            def squared_lo(i, f, cc, per, dst, hi):
                dve.wait_ge(mlp_hi, i * per + (8 * f + cc + 1))
                V.tensor_tensor(dst, SQ[cc % 2][:, :, :], hi.bitcast(fp32), ALU.subtract).then_inc(mlp_lo, 1)

            def down_rows(i, f, cc, per, cols):
                dve.wait_ge(piece_used, i * (8 * per) + (N0 + 64 * f + 32 + 8 * cc + 8))
                if f == 0 and cc == 0:
                    dve.wait_ge(rinv_squared, 1)
                bank = G[(cc + 1) % 2]
                for t in range(TILES):
                    v = X[:, t, cols]
                    V.scalar_tensor_tensor(out=v, in0=bank[:, t, :], scalar=rs[:, 3, t:t + 1], in1=v,
                                           op0=ALU.mult, op1=ALU.add).then_inc(x_added, 1)

            def gain_rows(cc):
                dve.wait_ge(nf_in, 16)
                for t in range(TILES):
                    dve.wait_ge(ss_ready, 10 + 2 * cc + t + 1)
                    v = X[:, t, 512 * cc:512 * cc + 512]
                    V.tensor_tensor(v, v, NF[:, 512 * cc:512 * cc + 512], ALU.mult).then_inc(gained, 1)

            for f in range(2):
                up0 = N0 + 64 * f
                for j in range(8):
                    if f or j >= 3:
                        mlp_split(0, up0, j, 0)
                    if j == 3 and f == 0:
                        dve.wait_ge(ss_ready, 2 + 8)
                        row_scales(1, 4)
                    if j == 0 and f == 1:
                        down_rows(0, 0, 3, 0, slice(1536, 2048))
                    if j == 4:
                        square(0, f, 0, 0)
                    if j == 5:
                        squared_lo(0, f, 0, 0, ML[:, 0:4, :], MH[:, 0:4, :])
                with dve.Fori(0, 3) as i:
                    for j in range(8):
                        mlp_split(i, up0 + 8, j, 8)
                        if j == 0:
                            square(i, f, 1, 2)
                        if j == 1:
                            squared_lo(i, f, 1, 2, ML[:, bass.ds(i * 8 + 4, 4), :], MH[:, bass.ds(i * 8 + 4, 4), :])
                        if j == 4:
                            square(i, f, 2, 2)
                        if j == 5:
                            squared_lo(i, f, 2, 2, ML[:, bass.ds(i * 8 + 8, 4), :], MH[:, bass.ds(i * 8 + 8, 4), :])
                dn0 = up0 + 32
                mlp_split(0, dn0, 0, 0)
                square(0, f, 7, 0)
                mlp_split(0, dn0, 1, 0)
                squared_lo(0, f, 7, 0, ML[:, 28:32, :], MH[:, 28:32, :])
                for j in range(2, 8):
                    mlp_split(0, dn0, j, 0)
                for cc in range(1, 4):
                    for j in range(8):
                        mlp_split(0, dn0 + 8 * cc, j, 0)
                        if j == 0:
                            down_rows(0, f, cc - 1, 0, slice(512 * (cc - 1), 512 * cc))
                        if j == 4 and f == 1:
                            gain_rows(cc - 1)
            down_rows(0, 1, 3, 0, slice(1536, 2048))
            dve.wait_ge(ss_ready, 18)
            row_scales(2, 4)
            for t in range(TILES):
                v = X[:, t, LAST]
                ins = V.scalar_tensor_tensor(out=v, in0=v, scalar=rs[:, 1, t:t + 1], in1=NF[:, LAST], op0=ALU.mult,
                                             op1=ALU.mult)
            ins.then_inc(normed_1, 1)
            dve.wait_ge(gained, 6)
            for cols in LEFT:
                v = X[:, 1, cols]
                V.tensor_scalar(v, v, rs[:, 1, 1:2], None, ALU.mult).then_inc(normed_1, 1)

        @block.tensor
        def _(pe):
            T_ = nc.tensor

            def mm(o_, l, r, start, stop):
                return T_.matmul(o_, l, r, start=start, stop=stop, skip_group_check=True)

            def three(o_, wh, wl, ah, al, start, stop, stationary):
                if stationary:
                    mm(o_, wh, ah, start, False)
                    mm(o_, wh, al, False, False)
                    return mm(o_, wl, ah, False, stop)
                mm(o_, ah, wh, start, False)
                mm(o_, ah, wl, False, False)
                return mm(o_, al, wh, False, stop)

            def norm_transposes():
                for kp in range(KT // 2):
                    if kp == 0:
                        pe.wait_ge(diag_ready, 2)
                    if kp >= 4:
                        pe.wait_ge(h_lo, 2 * (kp - 3))
                    for j in range(2):
                        for t in range(TILES):
                            k = 2 * kp + j
                            last = mm(TB[kp % 4][:, j * 256 + t * 128:j * 256 + (t + 1) * 128],
                                      X[:, t, k * 128:(k + 1) * 128], diag[:, t, :], True, True)
                    last.then_inc(h_tr, 1)

            def turn_x(c):
                pe.wait_ge(x_added, 2 * c + 2)
                for kp in range(2 * c, 2 * c + 2):
                    if c == 0:
                        pe.wait_ge(pT_out, 2 * HEADS)
                    if kp >= 4:
                        pe.wait_ge(h_lo, 16 + 2 * (kp - 3))
                    for j in range(2):
                        for t in range(TILES):
                            k = 2 * kp + j
                            last = T_.transpose(TB[kp % 4][:, j * 256 + t * 128:j * 256 + (t + 1) * 128],
                                                X[:, t, k * 128:(k + 1) * 128], ident)
                    last.then_inc(h_tr, 1)

            pe.wait_ge(oh_in, 16)
            pe.wait_ge(par_in, 16)
            table = oh[:, DIST_W + BIAS_W:]
            mm(G[0][0:HEADS, 0, 0:BIAS_W], table, oh[:, DIST_W:DIST_W + BIAS_W], True, True).then_inc(bias_mm, 1)

            for n in range(CMP_PAD):
                at_ = 512 + 128 - 16 * n - 31 if n < N_CMP else 0
                last = mm(G[1][:, 1, n * HEADS:(n + 1) * HEADS], oh[:, at_:at_ + 128], table, True, True)
            last.then_inc(bias_mm, 1)
            norm_transposes()
            pe.wait_ge(bias_row_ready, 1)

            def weights_tiles(s, no, k0, b, tiles, start, stop, moving=lambda part, k: (AH, AL)[part][:, k, :]):
                wh, wl = whi[no % 2], wlo[s % SLOTS]
                for k in range(4):
                    for m in tiles:
                        w = slice(512 * k + 128 * m, 512 * k + 128 * m + 128)
                        last = three(b[:, m // 2, (m % 2) * 256:(m % 2 + 1) * 256], wh[:, w], wl[:, w],
                                     moving(0, k0 + k), moving(1, k0 + k),
                                     start and k == 0 and m % 2 == 0, stop and k == 3, True)
                return last

            def row_tiles(s, no, ah, al, b, width, start, stop):
                wh, wl = whi[no % 2], wlo[s % SLOTS]
                for k in range(4):
                    for t in range(TILES):
                        w = slice(512 * k, 512 * k + 512) if width == 512 else slice(512 * k + 256, 512 * k + 512)
                        o_ = b[:, t, :] if width == 512 else b[:, 1, t * 256:(t + 1) * 256]
                        first = start and k == 0 and (width == 512 or t == 0)
                        last = three(o_, wh[:, w], wl[:, w], ah(k)[:, t * 128:(t + 1) * 128],
                                     al(k)[:, t * 128:(t + 1) * 128], first, stop and k == 3, False)
                return last

            for step, i in STEPS:
                if step == "product":
                    s = i
                    kind, c, g = STREAM[s]
                    if kind == "cmp":
                        pe.wait_ge(piece_in[s % SLOTS], 16 * (s // SLOTS + 1))
                        pe.wait_ge(flat_ready, c + 1)
                        for k in range(8):
                            kt = 8 * g + k
                            last = mm(hid_ps[:, 256 * c:256 * c + 256], flat[:, c, kt, :],
                                      raw[s % SLOTS][:, 256 * k:256 * k + 256], kt == 0, kt == 15)
                        last.then_inc(piece_used, 1)
                        continue
                    if kind == "glu":
                        no = split_no[s]
                        if s == G0:
                            pe.wait_ge(z_lo, 4)
                        if s == G0 + 2:
                            pe.wait_ge(sg_ready, 4)
                        pe.wait_ge(lo_ready, no + 1)
                        wh, wl = whi[no % 2], wlo[s % SLOTS]
                        for k in range(4):
                            for m in range(4):
                                w = slice(512 * k + 128 * m, 512 * k + 128 * m + 128)
                                last = three(G[1][:, m // 2, (m % 2) * 256:(m % 2 + 1) * 256], wh[:, w], wl[:, w],
                                             ZH[:, 4 * g + k, :], ZL[:, 4 * g + k, :],
                                             g == 0 and k == 0 and m % 2 == 0, g == 1 and k == 3, True)
                        last.then_inc(piece_used, 1)
                        continue
                    if kind == "out":
                        if c == 0 and g == 0:
                            pe.wait_ge(sg_ready, 8)
                            pe.wait_ge(mix_lo, 2)
                        if c == 1 and g == 0:
                            pe.wait_ge(lg_ready, 4 * HEADS)
                        if c >= 2 and g == out_first[c]:
                            pe.wait_ge(x_added, 2 * (c - 1))
                        if g >= 2:
                            pe.wait_ge(yt_lo, 4 * (g - 1))
                        pe.wait_ge(lo_ready, split_no[s] + 1)
                        row_tiles(s, split_no[s], lambda k: AH[:, 4 * g + k, :], lambda k: AL[:, 4 * g + k, :],
                                  G[(c + 1) % 2], 512, g == out_first[c], g == out_last[c]).then_inc(piece_used, 1)
                        continue
                    g_no = prod_no[(kind, c)]
                    b = G[g_no % 2]
                    if g == 0 and g_no == 1:
                        pe.wait_ge(biasc_ready, 3)
                    if g == 0 and g_no >= 2:
                        pe.wait_ge(*EVAC[g_no - 2])
                    if kind == "gate":
                        pe.wait_ge(lo_ready, split_no[s] + 1)
                        wh, wl = whi[split_no[s] % 2], wlo[s % SLOTS]
                        for k in range(KT):
                            w = slice(48 * k, 48 * k + 48)
                            last = three(b[0:48, 0, 0:256], wh[:, w], wl[:, w], AH[:, k, :], AL[:, k, :],
                                         k == 0, k == KT - 1, True)
                        last.then_inc(piece_used, 1)
                        continue
                    pe.wait_ge(lo_ready, split_no[s] + 1)
                    if g_no == 0:
                        pe.wait_ge(h_lo, 4 * g + 4)
                    no = split_no[s]
                    if c in (5, 6):
                        weights_tiles(s, no, 4 * g, b, range(2), g == 0, g == 3)
                        last = row_tiles(s, no, lambda k: AH[:, 4 * g + k, :], lambda k: AL[:, 4 * g + k, :],
                                         b, 256, g == 0, g == 3)
                    else:
                        last = weights_tiles(s, no, 4 * g, b, range(4), g == 0, g == 3)
                    last.then_inc(piece_used, 1)
                elif step == "x_T":
                    turn_x(i)
                elif step == "b_T":
                    pe.wait_ge(b_blocks, 4)
                    for r in range(2):
                        for j in range(2):
                            for q in range(4):
                                P0 = 4 * (4 * j + q)
                                last = T_.transpose(TB[2 * r + j][:, q * 128:(q + 1) * 128],
                                                    BD[:, r, P0:P0 + 4, :].rearrange("p a b -> p (a b)"), ident)
                            last.then_inc(b_T, 1)
                elif step == "bu":
                    k, q, r = i, i // 4, i % 4
                    pe.wait_ge(u_ready, q // 2 + 1)
                    if k == 0:
                        pe.wait_ge(b_T_out, 4)
                    if k >= 2:
                        pe.wait_ge(ssm_prod, 2 * (k - 1))
                    p = slice(32 * r, 32 * r + 32)
                    for j in range(2):
                        last = mm(BU[k % 2][:, j, :], BL[p, q, j, :], uT[p, q, :], True, True)
                    last.then_inc(bu_done, 1)
                elif step == "y":
                    k, q, r = i, i // 4, i % 4
                    pe.wait_ge(ssm_state, 2 * k + 2)
                    if k == 0:
                        pe.wait_ge(c_blocks, 4)
                    if r == 0 and q >= 1:
                        pe.wait_ge(y_out, q)
                    o_ = YB[32 * r:32 * r + 32, (q % 2) * 256:(q % 2 + 1) * 256]
                    mm(o_, CL[:, 0, k, :], S[k % 2][:, 0, :], True, False)
                    mm(o_, CL[:, 1, k, :], S[k % 2][:, 1, :], False, True).then_inc(y_done, 1)
                elif step == "cmp_kv":
                    pe.wait_ge(hid_ready, 3)
                    for j in range(2):
                        last = mm(kc_ps, P("w2k")[:, 128 * j:128 * j + 128],
                                  hidk[:, j, :, :].rearrange("p v n -> p (v n)"), j == 0, j == 1)
                    last.then_inc(cmp_kv, 1)
                    for v in range(KV):
                        for j in range(2):
                            hv = hidv[:, j, v, :, :].rearrange("p r n -> p (r n)")
                            last = mm(vc_ps[:, v, :], hv, P("w2v")[:, 64 * j:64 * j + 64], j == 0, j == 1)
                    last.then_inc(cmp_kv, 1)
                elif step == "cmp_l":
                    pe.wait_ge(cmp_kv_out, 7)
                    pe.wait_ge(q_ready, 4)
                    for t in range(TILES):
                        for m in range(HEADS // 2):
                            col = (t * HEADS // 2 + m) * 2 * CMP_PAD
                            last = mm(OB[:, col:col + 2 * CMP_PAD], qT[:, m, t * 128:(t + 1) * 128],
                                      kcmp[:, m // 2, :], True, True)
                    last.then_inc(cmp_logits, 1)
                elif step == "cmp_T":
                    pe.wait_ge(cmp_step, 8)
                    pe.wait_ge(kv_ready, 5)
                    for t in range(TILES):
                        for v in range(KV):
                            k0 = t * HEADS + 4 * v
                            last = T_.transpose(G[0][:, t, v * 128:(v + 1) * 128],
                                                pcmp[:, k0:k0 + 4, :].rearrange("p h n -> p (h n)"), ident)
                    last.then_inc(cmp_T, 1)
                elif step == "gate_T":
                    pe.wait_ge(gate_T, 1)
                    for t in range(TILES):
                        last = T_.transpose(G[1][:, 1, 48 * t:48 * t + 48], gatesT[:, t * 128:(t + 1) * 128],
                                            ident[0:48, 0:48])
                    last.then_inc(gate_T, 1)
                elif step == "hid_T":
                    pe.wait_ge(hrow_ready, 1)
                    for j in range(4):
                        last = T_.transpose(OB[:, 64 * j:64 * j + 64], hrow[:, 128 * j:128 * j + 128],
                                            ident[0:64, 0:64])
                    last.then_inc(hid_T, 1)
                elif step == "qk":
                    h, v = i, i // 4
                    p = slice(64 * (h % 2), 64 * (h % 2) + 64)
                    if h == 0:
                        pe.wait_ge(kv_ready, 10)
                        pe.wait_ge(cmp_T_out, 2)
                    else:
                        pe.wait_ge(lg_ready, 4 * h)
                    for a in range(2):
                        mm(G[0][:, a, 0:256], qT[p, h // 2, 128:256], kdup[a][p, v, :], True, True)
                        last = mm(G[0][:, a, 256:384], qT[p, h // 2, 0:128], kdup[a][p, v, 0:128], True, True)
                    last.then_inc(qk_done, 1)
                elif step == "pT":
                    h = i
                    if h == 0:
                        pe.wait_ge(ssm_prod, 2 * PAIRS)
                    else:
                        pe.wait_ge(pT_out, 2 * h)
                    pe.wait_ge(diag_out, h + 1)
                    for a in range(2):
                        for j, (src, t) in enumerate(((2, 0), (0, 1), (1, 1))):
                            last = mm(TB[a][:, j * 128:(j + 1) * 128], prob[h % 2][:, a, src * 128:(src + 1) * 128],
                                      dg[h % 2][:, 2 * a + t, :], True, True)
                        last.then_inc(pT_done, 1)
                elif step == "pv":
                    h, v, pair = i, i // 4, i // 2
                    y = YT[pair % 2]
                    if h % 2 == 0:
                        if pair == 0:
                            pe.wait_ge(cmp_T_out, 2)
                            pe.wait_ge(cmp_step, 1)
                        elif pair == 1:
                            pe.wait_ge(y_out, OCTETS)
                        else:
                            pe.wait_ge(yt_lo, pair - 1)
                        mm(y, vblk[:, v, 128 * (pair % 2):128 * (pair % 2) + 128],
                           pcT[:, v, :, :].rearrange("p t q -> p (t q)"), True, False)
                    pe.wait_ge(pT_out, 2 * h + 2)
                    o_ = y[64 * (h % 2):64 * (h % 2) + 64, :]
                    for a in range(2):
                        cols = slice(v * HD, (v + 1) * HD)
                        mm(o_, vrow[a][:, 0, cols], pT[h % 2][:, a, 0:256], False, False)
                        last = mm(o_[:, 128:256], vrow[a][:, 1, cols], pT[h % 2][:, a, 256:384], False,
                                  a == 1 and h % 2 == 1)
                    last.then_inc(pv_done, 1)

            for f in range(2):
                up0 = N0 + 64 * f
                sp0 = SP0 + 64 * f

                def up_chunk(i, c, per):
                    for g in range(4):
                        j = 4 * c + g
                        pe.wait_ge(lo_ready, i * (4 * per) + (sp0 + j + 1))
                        if f == 0 and c == 0 and per == 0:
                            pe.wait_ge(h_lo, 16 + 4 * g + 4)
                        weights_tiles(up0 + j, sp0 + j, 4 * g, G[(c + 1) % 2], range(4), g == 0, g == 3,
                                      h2).then_inc(piece_used, 1)
                        if f == 0 and c == 0 and per == 0 and g == 0:
                            turn_x(3)

                for c in range(2):
                    if f:
                        pe.wait_ge(x_added, 8 + 8 * f - 2 + 2 * c)
                    up_chunk(0, c, 0)
                with pe.Fori(0, 3) as i:
                    for c in range(2):
                        pe.wait_ge(relu_ready, i * 2 + (8 * f + c + 1))
                        up_chunk(i, 2 + c, 2)

                def down_chunk(i, c, per, last_up):
                    for g in range(8):
                        j = 32 + 8 * c + g
                        pe.wait_ge(lo_ready, i * (8 * per) + (sp0 + j + 1))
                        if last_up and g == 7:
                            pe.wait_ge(mlp_lo, 8 * f + 8)
                        row_tiles(up0 + j, sp0 + j, lambda k: MH[:, 4 * g + k, :], lambda k: ML[:, 4 * g + k, :],
                                  G[(c + 1) % 2], 512, g == 0, g == 7).then_inc(piece_used, 1)

                for c in range(2):
                    pe.wait_ge(relu_ready, 8 * f + 7 + c)
                    if c == 0:
                        pe.wait_ge(mlp_lo, 8 * f + 7)
                    down_chunk(0, c, 0, c == 0)
                for c in range(2):
                    pe.wait_ge(x_added, 8 + 8 * f + 2 * c + 2)
                    down_chunk(0, 2 + c, 0, False)


COEF_N = 25


def _buckets():
    dist = np.arange(0, SEQ)
    exact = BUCKETS // 2
    large = exact + (np.log(np.maximum(dist, 1).astype(np.float32) / exact)
                     / np.float32(math.log(MAX_DIST / exact)) * (BUCKETS - exact)).astype(np.int32)
    b = np.where(dist < exact, dist, np.minimum(large, BUCKETS - 1))
    hot = np.zeros((BUCKETS + 1, DIST_W + BIAS_W), np.float32)
    for m in range(DIST_W):
        hot[b[m - 512] if m >= 512 else BUCKETS, m] = 1.0
    for j in range(BIAS_W):
        hot[b[255 - j] if j <= 255 else BUCKETS, DIST_W + j] = 1.0
    return hot


def kernel(**inputs):
    import concourse.bacc as bacc
    from concourse.bass_utils import run_bass_kernel_spmd

    a = {k: np.asarray(v) for k, v in inputs.items()}

    def pairs(v):
        v = v.reshape(PAIRS, 2, 64, *v.shape[2:])
        return np.moveaxis(v, 0, 2).reshape(128, PAIRS, *v.shape[3:])

    def columns(v):
        return v.reshape(-1, 128).T

    group, state = a["ssm_a_re"].shape[1:]
    rows = np.arange(128)[:, None]
    parts = {
        "n1": columns(a["norm1_w"][0]), "n2": columns(a["norm2_w"][0]),
        "are": pairs(a["ssm_a_re"][0]), "aim": pairs(a["ssm_a_im"][0]),
        "ldt": pairs(np.broadcast_to(a["ssm_log_dt"][0][:, None], (group, state))),
        "d": columns(a["ssm_d"][0].reshape(-1)), "bglu": columns(a["b_glu"][0]),
        "pek": columns(a["pe_ck"][0].reshape(-1)), "pev": columns(a["pe_cv"][0].reshape(-1)),
        "w2k": np.repeat(a["w_ck2"][0].reshape(2, 128, 1, 64), 2, 2).transpose(1, 0, 2, 3).reshape(128, 256),
        "w2v": a["w_cv2"][0].reshape(2, 128, 64).transpose(1, 0, 2).reshape(128, 128),
        "tv": np.broadcast_to(np.arange(SEQ, dtype=np.float32), (128, SEQ)),
        "ident": np.eye(128, dtype=np.float32),
        "valid": np.concatenate([rows >= 31, rows >= 0], 1).astype(np.float32),
    }
    params = np.concatenate([parts[n] for n in PACK], axis=1)
    bc = np.stack([pairs(a["ssm_b_re"][0]), pairs(a["ssm_b_im"][0]),
                   pairs(a["ssm_c_re"][0].transpose(0, 2, 1)), pairs(a["ssm_c_im"][0].transpose(0, 2, 1))], 1)
    table = np.concatenate([a["rel_table"], np.full((1, HEADS), NEG, np.float32)], 0)
    arrays = {
        "x": a["x"][0], "w_in": a["w_in"][0], "w_glu": a["w_glu"][0], "w_out": a["w_out"][0],
        "w_up": a["w_up"][0], "w_down": a["w_down"][0], "w_ck1": a["w_ck1"][0], "w_cv1": a["w_cv1"][0],
        "nf": a["norm_f_w"], "params": params, "bc": bc.reshape(128, -1),
        "buckets": np.concatenate([_buckets(), table], 1),
    }
    nc = bacc.Bacc("TRN2", target_bir_lowering=False, num_devices=1)
    args, feed = [], {}
    for name, v in arrays.items():
        feed["in_" + name] = np.ascontiguousarray(v)
        args.append(nc.dram_tensor("in_" + name, v.shape, mybir.dt.float32, kind="ExternalInput").ap())
    out = nc.dram_tensor("out_0", (SEQ, D), mybir.dt.float32, kind="ExternalOutput").ap()
    hybrid_layer(nc, *args, out)
    got = run_bass_kernel_spmd(nc, [feed], core_ids=[0])
    return got.results[0]["out_0"].reshape(1, SEQ, D)
```
